# Optimizing a Trainium2 kernel written in Bass

```python
import math
import jax, jax.numpy as jnp
from jax import lax
import numpy as np

D_MODEL = 2048
BATCH = 1
SEQ = 256
DEPTH = 1

GRID_W = 64
CTX_LEN = 256
MIX_W = D_MODEL
GDN_W = MIX_W // 2
HYENA_W = MIX_W - GDN_W
GDN_HEADS = 8
GDN_HEAD_DIM = GDN_W // GDN_HEADS
GDN_CONV = 5
GDN_CHUNK = 64
HYENA_CONV = 3
HYENA_EMB = 33
HYENA_FILTER_W = 64
HYENA_DECAY_TARGET = 1e-2
HYENA_FAST_PCT = 0.3
HYENA_SLOW_PCT = 1.5
D_FF = ((8 * D_MODEL // 3 + 255) // 256) * 256
EPS = 1e-6

COL_K = 0
COL_V = COL_K + GDN_W
COL_Q = COL_V + GDN_W
COL_BETA = COL_Q + GDN_W
COL_Z = COL_BETA + 4 * GDN_HEADS
COL_HY = COL_Z + GDN_W
IN_COLS = COL_HY + 3 * HYENA_W

kernel_name = "hybrid_gdn_hyena_prefix_dit_block"

def _rmsnorm(x, g):
    xf = x.astype(jnp.float32)
    y = xf * lax.rsqrt(jnp.mean(xf * xf, axis=-1, keepdims=True) + EPS)
    return (y * g.astype(jnp.float32)).astype(x.dtype)

def _l2norm(x):
    xf = x.astype(jnp.float32)
    return xf * lax.rsqrt(jnp.sum(xf * xf, axis=-1, keepdims=True) + EPS)

def _dwconv(u, w):
    K = w.shape[0]
    pad = K // 2
    L = u.shape[1]
    up = jnp.pad(u, ((0, 0), (pad, pad), (0, 0)))
    out = up[:, 0:L] * w[0]
    for i in range(1, K):
        out = out + up[:, i:i + L] * w[i]
    return out

def _adaln(cvec, w_mod, b_mod):
    m = jax.nn.silu(cvec) @ w_mod + b_mod
    return jnp.split(m[..., None, :], 6, axis=-1)

def _heads(t):
    return t.reshape(t.shape[:-1] + (GDN_HEADS, GDN_HEAD_DIM))

def _gdn_gates(ba, a_log, dt_bias):
    ba = ba.astype(jnp.float32).reshape(ba.shape[:-1] + (2, 2, GDN_HEADS))
    beta = jax.nn.sigmoid(ba[..., 0, :, :])
    g = -jnp.exp(a_log.astype(jnp.float32)) * jax.nn.softplus(ba[..., 1, :, :] + dt_bias.astype(jnp.float32))
    return beta, g

def _to_chunks(t):
    B, L, H = t.shape[:3]
    t = t.reshape((B, L // GDN_CHUNK, GDN_CHUNK, H) + t.shape[3:])
    return jnp.moveaxis(t, (1, 3), (0, 2))

def _gdn_chunks(k, v, beta, g):
    kc, vc, bc, gc = _to_chunks(k), _to_chunks(v), _to_chunks(beta), _to_chunks(g)
    gcum = jnp.cumsum(gc, axis=-1)
    idx = jnp.arange(GDN_CHUNK)
    strict = idx[:, None] > idx[None, :]
    diff = jnp.where(strict, gcum[..., :, None] - gcum[..., None, :], 0.0)
    kk = jnp.einsum('nbhid,nbhjd->nbhij', kc, kc)
    a_strict = jnp.where(strict, bc[..., :, None] * kk * jnp.exp(diff), 0.0)
    lower_unit = a_strict + jnp.eye(GDN_CHUNK, dtype=a_strict.dtype)
    rhs = jnp.concatenate([vc * bc[..., None], kc * (bc * jnp.exp(gcum))[..., None]], axis=-1)
    sol = lax.linalg.triangular_solve(lower_unit, rhs, left_side=True, lower=True, unit_diagonal=True)
    dv = vc.shape[-1]
    return kc, gcum, sol[..., :dv], sol[..., dv:]

def _gdn_scan(kc, gcum, u, w, s0, emit):
    def step(s, xs):
        k_n, g_n, u_n, w_n = xs
        v_new = u_n - jnp.einsum('bhcd,bhde->bhce', w_n, s)
        g_last = g_n[..., -1]
        s_next = s * jnp.exp(g_last)[..., None, None] + jnp.einsum(
            'bhcd,bhce->bhde', k_n * jnp.exp(g_last[..., None] - g_n)[..., None], v_new)
        return s_next, ((s, v_new) if emit else None)
    return lax.scan(step, s0, (kc, gcum, u, w))

def _gdn_direction(q, k, v, beta, g, s0):
    kc, gcum, u, w = _gdn_chunks(k, v, beta, g)
    s_fin, (s_start, v_new) = _gdn_scan(kc, gcum, u, w, s0, True)
    qc = _to_chunks(q)
    idx = jnp.arange(GDN_CHUNK)
    incl = idx[:, None] >= idx[None, :]
    diff = jnp.where(incl, gcum[..., :, None] - gcum[..., None, :], 0.0)
    attn = jnp.where(incl, jnp.einsum('nbhid,nbhjd->nbhij', qc, kc) * jnp.exp(diff), 0.0)
    o = (jnp.einsum('nbhcd,nbhde->nbhce', qc * jnp.exp(gcum)[..., None], s_start)
         + jnp.einsum('nbhij,nbhje->nbhie', attn, v_new))
    N, B, H, C, E = o.shape
    return jnp.moveaxis(o, (0, 2), (1, 3)).reshape(B, N * C, H, E), s_fin

def _gdn_final_state(k, v, beta, g, s0):
    kc, gcum, u, w = _gdn_chunks(k, v, beta, g)
    s_fin, _ = _gdn_scan(kc, gcum, u, w, s0, False)
    return s_fin

def _hyena_filter(L, w1, b1, f1, w2, b2, f2, w3, b3, f3, w4):
    f32 = jnp.float32
    t = jnp.arange(L, dtype=f32)
    t01 = t / max(L - 1, 1)
    bands = (HYENA_EMB - 1) // 2
    freqs = jnp.linspace(1e-4, bands - 1, bands, dtype=f32)
    ang = (2.0 * math.pi / L) * t[:, None] * freqs[None, :]
    z = jnp.concatenate([t01[:, None], jnp.cos(ang), -jnp.sin(ang)], axis=-1)
    h = jnp.sin(f1.astype(f32) * (z @ w1.astype(f32) + b1.astype(f32)))
    h = jnp.sin(f2.astype(f32) * (h @ w2.astype(f32) + b2.astype(f32)))
    h = jnp.sin(f3.astype(f32) * (h @ w3.astype(f32) + b3.astype(f32)))
    h = h @ w4.astype(f32)
    max_decay = math.log(HYENA_DECAY_TARGET) / HYENA_FAST_PCT
    min_decay = math.log(HYENA_DECAY_TARGET) / HYENA_SLOW_PCT
    deltas = jnp.abs(jnp.linspace(min_decay, max_decay, HYENA_W, dtype=f32))
    window = jnp.exp(-t01[:, None] * deltas[None, :])
    return h * jnp.tile(window, (1, 2))

def _long_conv_bidir(u, filt):
    L, C = u.shape[1], u.shape[2]
    hf, hb = filt[:, :C], filt[:, C:]
    taps = jnp.concatenate([hf, jnp.zeros((1, C), filt.dtype), hb[:0:-1]], axis=0)
    U = jnp.fft.rfft(u.astype(jnp.float32), n=2 * L, axis=1)
    K = jnp.fft.rfft(taps, n=2 * L, axis=0)
    y = jnp.fft.irfft(U * K[None], n=2 * L, axis=1)[:, :L]
    return y.astype(u.dtype)

def _mixer(h, s0_f, s0_b, p):
    B, L, _ = h.shape
    proj = h @ p['w_in']
    qkv = jax.nn.silu(_dwconv(proj[..., COL_K:COL_BETA], p['conv_qkv']))
    k = _l2norm(_heads(qkv[..., COL_K:COL_V]))
    v = _heads(qkv[..., COL_V:COL_Q]).astype(jnp.float32)
    q = _l2norm(_heads(qkv[..., COL_Q:COL_BETA])) * (GDN_HEAD_DIM ** -0.5)
    beta, g = _gdn_gates(proj[..., COL_BETA:COL_Z], p['a_log'], p['dt_bias'])
    o_f, s_f = _gdn_direction(q, k, v, beta[:, :, 0], g[:, :, 0], s0_f)
    o_b, s_b = _gdn_direction(jnp.flip(q, 1), jnp.flip(k, 1), jnp.flip(v, 1),
                              jnp.flip(beta[:, :, 1], 1), jnp.flip(g[:, :, 1], 1), s0_b)
    z = jax.nn.silu(_heads(proj[..., COL_Z:COL_HY]).astype(jnp.float32))
    o = _rmsnorm(o_f + jnp.flip(o_b, 1), p['gdn_norm']) * z
    o = o.reshape(B, L, GDN_W).astype(h.dtype)
    hy = _dwconv(proj[..., COL_HY:], p['conv_hy']) + p['conv_hy_b']
    x0, x1, vh = jnp.split(hy, 3, axis=-1)
    uh = x1 * vh
    filt = _hyena_filter(L, p['filt_w1'], p['filt_b1'], p['filt_freq1'], p['filt_w2'], p['filt_b2'],
                         p['filt_freq2'], p['filt_w3'], p['filt_b3'], p['filt_freq3'], p['filt_w4'])
    y = x0 * (_long_conv_bidir(uh, filt) + p['hyena_bias'] * uh)
    out = jnp.concatenate([o, y], axis=-1) @ p['w_out']
    return out, s_f, s_b

def _block(s, mod, s0_f, s0_b, p):
    sh_a, sc_a, g_a, sh_f, sc_f, g_f = mod
    h = _rmsnorm(s, p['norm_pre_mix']) * (1.0 + sc_a) + sh_a
    out, s_f, s_b = _mixer(h, s0_f, s0_b, p)
    s = s + g_a * _rmsnorm(out, p['norm_post_mix'])
    h = _rmsnorm(s, p['norm_pre_ffn']) * (1.0 + sc_f) + sh_f
    ff = (jax.nn.silu(h @ p['w_gate']) * (h @ p['w_up'])) @ p['w_down']
    s = s + g_f * _rmsnorm(ff, p['norm_post_ffn'])
    return s, s_f, s_b

def _context_states(ctx, mod, p):
    sh_a, sc_a = mod[0], mod[1]
    h = _rmsnorm(ctx, p['norm_pre_mix']) * (1.0 + sc_a) + sh_a
    kv = jax.nn.silu(_dwconv(h @ p['w_in'][:, COL_K:COL_Q], p['conv_qkv'][:, COL_K:COL_Q]))
    k = _l2norm(_heads(kv[..., :GDN_W]))
    v = _heads(kv[..., GDN_W:]).astype(jnp.float32)
    beta, g = _gdn_gates(h @ p['w_in'][:, COL_BETA:COL_Z], p['a_log'], p['dt_bias'])
    s0 = jnp.zeros((ctx.shape[0], GDN_HEADS, GDN_HEAD_DIM, GDN_HEAD_DIM), jnp.float32)
    s_f = _gdn_final_state(k, v, beta[:, :, 0], g[:, :, 0], s0)
    s_b = _gdn_final_state(jnp.flip(k, 1), jnp.flip(v, 1), jnp.flip(beta[:, :, 1], 1), jnp.flip(g[:, :, 1], 1), s0)
    return s_f, s_b

def setup_inputs(seed: int = 0) -> dict:
    key = jax.random.key(seed)
    ks = jax.random.split(key, 34)
    f32 = jnp.float32
    D, NL = D_MODEL, DEPTH

    def nrm(k, shape, scale):
        return jax.random.normal(k, shape, f32) * scale

    dt = jnp.exp(jax.random.uniform(ks[13], (NL, 2, GDN_HEADS), f32, math.log(1e-3), math.log(1e-1)))
    return {
        'x': nrm(ks[0], (BATCH, SEQ, D), 1.0),
        'c': nrm(ks[1], (BATCH, D), 1.0),
        'ctx': nrm(ks[2], (BATCH, CTX_LEN, D), 1.0),
        'c_ctx': nrm(ks[3], (D,), 1.0),
        'w_mod': nrm(ks[4], (NL, D, 6 * D), 0.5 * D ** -0.5),
        'b_mod': nrm(ks[5], (NL, 6 * D), 0.02),
        'norm_pre_mix': 1.0 + nrm(ks[6], (NL, D), 0.05),
        'norm_post_mix': 1.0 + nrm(ks[7], (NL, D), 0.05),
        'norm_pre_ffn': 1.0 + nrm(ks[8], (NL, D), 0.05),
        'norm_post_ffn': 1.0 + nrm(ks[9], (NL, D), 0.05),
        'w_in': nrm(ks[10], (NL, D, IN_COLS), D ** -0.5),
        'conv_qkv': nrm(ks[11], (NL, GDN_CONV, 3 * GDN_W), GDN_CONV ** -0.5),
        'a_log': jnp.log(jax.random.uniform(ks[12], (NL, 2, GDN_HEADS), f32, 1.0, 16.0)),
        'dt_bias': dt + jnp.log(-jnp.expm1(-dt)),
        'gdn_norm': 1.0 + nrm(ks[14], (NL, GDN_HEAD_DIM), 0.05),
        'conv_hy': nrm(ks[15], (NL, HYENA_CONV, 3 * HYENA_W), HYENA_CONV ** -0.5),
        'conv_hy_b': nrm(ks[16], (NL, 3 * HYENA_W), 0.02),
        'filt_w1': nrm(ks[17], (NL, HYENA_EMB, HYENA_FILTER_W), HYENA_EMB ** -0.5),
        'filt_b1': nrm(ks[18], (NL, HYENA_FILTER_W), 0.02),
        'filt_freq1': 1.0 + nrm(ks[19], (NL, HYENA_FILTER_W), 0.05),
        'filt_w2': nrm(ks[20], (NL, HYENA_FILTER_W, HYENA_FILTER_W), HYENA_FILTER_W ** -0.5),
        'filt_b2': nrm(ks[21], (NL, HYENA_FILTER_W), 0.02),
        'filt_freq2': 1.0 + nrm(ks[22], (NL, HYENA_FILTER_W), 0.05),
        'filt_w3': nrm(ks[23], (NL, HYENA_FILTER_W, HYENA_FILTER_W), HYENA_FILTER_W ** -0.5),
        'filt_b3': nrm(ks[24], (NL, HYENA_FILTER_W), 0.02),
        'filt_freq3': 1.0 + nrm(ks[25], (NL, HYENA_FILTER_W), 0.05),
        'filt_w4': nrm(ks[26], (NL, HYENA_FILTER_W, 2 * HYENA_W), 0.02),
        'hyena_bias': nrm(ks[27], (NL, HYENA_W), 1.0),
        'w_out': nrm(ks[28], (NL, MIX_W, D), MIX_W ** -0.5),
        'w_gate': nrm(ks[29], (NL, D, D_FF), D ** -0.5),
        'w_up': nrm(ks[30], (NL, D, D_FF), D ** -0.5),
        'w_down': nrm(ks[31], (NL, D_FF, D), D_FF ** -0.5),
    }

def reference(x, c, ctx, c_ctx, w_mod, b_mod, norm_pre_mix, norm_post_mix, norm_pre_ffn, norm_post_ffn,
              w_in, conv_qkv, a_log, dt_bias, gdn_norm, conv_hy, conv_hy_b,
              filt_w1, filt_b1, filt_freq1, filt_w2, filt_b2, filt_freq2, filt_w3, filt_b3, filt_freq3, filt_w4,
              hyena_bias, w_out, w_gate, w_up, w_down):
    for layer in range(DEPTH):
        p = {
            'norm_pre_mix': norm_pre_mix[layer], 'norm_post_mix': norm_post_mix[layer],
            'norm_pre_ffn': norm_pre_ffn[layer], 'norm_post_ffn': norm_post_ffn[layer],
            'w_in': w_in[layer], 'conv_qkv': conv_qkv[layer], 'a_log': a_log[layer], 'dt_bias': dt_bias[layer],
            'gdn_norm': gdn_norm[layer], 'conv_hy': conv_hy[layer], 'conv_hy_b': conv_hy_b[layer],
            'filt_w1': filt_w1[layer], 'filt_b1': filt_b1[layer], 'filt_freq1': filt_freq1[layer],
            'filt_w2': filt_w2[layer], 'filt_b2': filt_b2[layer], 'filt_freq2': filt_freq2[layer],
            'filt_w3': filt_w3[layer], 'filt_b3': filt_b3[layer], 'filt_freq3': filt_freq3[layer],
            'filt_w4': filt_w4[layer], 'hyena_bias': hyena_bias[layer], 'w_out': w_out[layer],
            'w_gate': w_gate[layer], 'w_up': w_up[layer], 'w_down': w_down[layer],
        }
        mod_x = _adaln(c, w_mod[layer], b_mod[layer])
        mod_c = _adaln(c_ctx[None], w_mod[layer], b_mod[layer])
        if layer + 1 < DEPTH:
            s0 = jnp.zeros((ctx.shape[0], GDN_HEADS, GDN_HEAD_DIM, GDN_HEAD_DIM), jnp.float32)
            ctx, s_f, s_b = _block(ctx, mod_c, s0, s0, p)
        else:
            s_f, s_b = _context_states(ctx, mod_c, p)
        x, _, _ = _block(x, mod_x, s_f, s_b, p)
    return x


_drawn_inputs = setup_inputs


def setup_inputs(seed=0):
    import zlib

    import numpy as np

    out = dict(_drawn_inputs(seed))
    spreads = {}
    factors = {'ctx': 4.404,
     'c_ctx': 7.879,
     'norm_post_mix': 3.475,
     'norm_pre_ffn': 2.855,
     'norm_post_ffn': 3.787,
     'gdn_norm': 8.0,
     'conv_hy_b': 5.956,
     'filt_b1': 8.0,
     'filt_freq1': 8.0,
     'filt_b2': 8.0,
     'filt_freq2': 8.0,
     'filt_b3': 8.0,
     'filt_freq3': 8.0}
    for name, (base, spread) in spreads.items():
        noise = np.random.default_rng([zlib.crc32(name.encode()), seed]).standard_normal(out[name].shape)
        drawn = base * np.exp(spread * noise) if base else spread * noise
        out[name] = __import__('jax').numpy.asarray(drawn.astype(out[name].dtype))
    for name, factor in factors.items():
        out[name] = (out[name] * factor).astype(out[name].dtype)
    return out
```

```python
from contextlib import ExitStack

import numpy as np

import concourse.bass as bass
from concourse import mybir

F32 = mybir.dt.float32
F32R = mybir.dt.float32r
BF16 = mybir.dt.bfloat16
I32 = mybir.dt.int32
ALU = mybir.AluOpType
ACT = mybir.ActivationFunctionType

P = 128
D = 2048
KT_N = D // P
SEQ = 256
TOK = 512
CH = 128
NCHUNK = TOK // CH
HEADS = 8
HD = 128
HY_CH = 1024
FF = 5632
FF_T = FF // P
EPS = 1e-6
KW, HW_ = 5, 3
EMB = 33
FW = 64
PI_IN = float(np.nextafter(np.float32(np.pi), np.float32(0)))
TWO_PI = (6.28125, float(np.float32(round((2 * np.pi - 6.28125) * 2 ** 20) / 2 ** 20)))
TWO_PI += (2 * np.pi - sum(TWO_PI),)
TILE = 2048
ORDER = ((2, 3, 0, 1), (3, 2, 1, 0))
LEVELS = (1, 2, 4, 8, 16, 32, 64)

RAW_SLOTS, SPLIT_SLOTS = 3, 2
RAW_OF_HEAD = [0, 1, 2, 0, 1, 2, 1]
RAW_OF_4 = [0, 1, 2, 1]


class Phase:

    def __init__(self, name, n, iters, raw=None, split=None):
        self.name, self.n, self.iters = name, n, iters
        self.raw = raw or [j % RAW_SLOTS for j in range(n)]
        self.split = split or [j % SPLIT_SLOTS for j in range(n)]


class Stream:

    def __init__(self, phases):
        self.phases, base = {p.name: p for p in phases}, 0
        raw, split = [], []
        for p in phases:
            p.base = base
            raw += p.raw * p.iters
            split += p.split * p.iters
            base += p.n * p.iters
        self.raw, self.splits = raw, split
        self.total = base

    def tile(self, p, i, j):
        return p.base + p.n * i + j

    def gap(self, slots, t):
        return next((t - u for u in range(t - 1, -1, -1) if slots[u] == slots[t]), None)

    def free(self, slots, p, i, j):
        if isinstance(i, int):
            g = self.gap(slots, self.tile(p, i, j))
        else:
            g = min(self.gap(slots, self.tile(p, n, j)) for n in range(p.iters))
        return None if g is None else self.tile(p, i, j) - g + 1

    def plan(self):
        self.release = []
        for u in range(self.total):
            v = next((v for v in range(u - 1, -1, -1) if self.splits[v] == self.splits[u]), -1)
            self.release.append(max([v] + self.release[-1:]))

    def at(self, t):
        p = next(p for p in reversed(list(self.phases.values())) if t >= p.base)
        return p, (t - p.base) // p.n, (t - p.base) % p.n

    def refill(self, p, i, j):
        if isinstance(i, int):
            t = self.tile(p, i, j)
            return [self.at(u) for u in range(t + 1, min(t + 3, self.total)) if self.release[u] == t]
        found = None
        for n in range(p.iters - 1):
            t = self.tile(p, n, j)
            ahead = [u - t for u in range(t + 1, t + 3) if self.release[u] == t]
            if found is None:
                found = ahead
            if found != ahead:
                raise ValueError(f"{p.name}: tile {j} is followed by {found} and {ahead}")
        return [(p, i + (j + a) // p.n, (j + a) % p.n) for a in found]

    def landed(self, p, i, j):
        s = p.raw[j]
        before = sum(1 for t in range(p.base) if self.raw[t] == s)
        return 16 * (before + p.raw.count(s) * i + p.raw[:j + 1].count(s))


def levels_mask():
    i, j = np.arange(CH)[:, None], np.arange(CH)[None, :]
    return np.stack([((i // (2 * s)) == (j // (2 * s))) & ((i // s) % 2 == 1) & ((j // s) % 2 == 0) for s in LEVELS])


def host_constants():
    f = np.float32
    i, j = np.arange(P)[:, None], np.arange(P)[None, :]
    c = {}
    m = levels_mask()
    c["c_lev"] = np.stack([m, m.transpose(0, 2, 1)]).transpose(2, 0, 1, 3).astype(f).copy()
    c["c_sq"] = np.stack([i == j, i <= j, i >= j, np.ones((P, P), bool)]).transpose(1, 0, 2).astype(f).copy()
    t = np.arange(SEQ, dtype=np.float64)[:, None]
    w = 2 * np.pi * (np.arange(SEQ, dtype=np.float64)[None, :] + 0.5) / (2 * SEQ)
    C, S = np.cos(t * w), np.sin(t * w)
    tile = lambda a: a.astype(f).reshape(2, P, SEQ).transpose(1, 0, 2)
    c["c_dft"] = np.stack([tile(C), tile(S), tile(C.T / SEQ), tile(-S.T / SEQ)], axis=1).copy()
    t32 = np.arange(SEQ, dtype=f)
    t01 = (t32 / f(SEQ - 1)).astype(f)
    bands = (EMB - 1) // 2
    freqs = np.linspace(1e-4, bands - 1, bands, dtype=f)
    ang = (f(2.0 * np.pi / SEQ) * t32[:, None] * freqs[None, :]).astype(f)
    z = np.concatenate([t01[:, None], np.cos(ang), -np.sin(ang)], axis=-1).astype(f)
    c["c_pos"] = z.T.copy()
    hi, lo = np.log(1e-2) / 0.3, np.log(1e-2) / 1.5
    deltas = np.abs(np.linspace(lo, hi, HY_CH, dtype=f))
    win = np.exp(-t01[:, None] * deltas[None, :]).astype(f)
    c["c_win"] = win.reshape(2, P, HY_CH).transpose(1, 0, 2).copy()
    return c


def build(nc, A, out):
    ctx = ExitStack()
    with ctx:
        base0 = (nc.sbuf_base + 63) // 64 * 64
        KB = 1024

        def at(name, kb, shape, dt=F32):
            return nc.alloc_sbuf_tensor_at(name, shape, dt, offset=base0 + int(kb * KB))

        def sem(name):
            return ctx.enter_context(nc.semaphore(name))

        hh = at("h_hi", 0, [P, KT_N, TOK], F32R)
        hl = at("h_lo", 32, [P, KT_N, TOK], F32R)
        raw = [at(f"w_raw{s}", 64 + 8 * s, [P, TILE]) for s in range(RAW_SLOTS)]
        whi = [at(f"w_hi{s}", 88 + 8 * s, [P, TILE], F32R) for s in range(SPLIT_SLOTS)]
        wlo = [at(f"w_lo{s}", 104 + 8 * s, [P, TILE], F32R) for s in range(SPLIT_SLOTS)]
        lev = at("lev", 120, [P, 2, 7, P], BF16)
        levf = at("lev_f32", 140, [P, 2, 7, P])
        sq = at("squares", 124, [P, 4, P])
        tabs = at("tabs", 126, [P, 6, NCHUNK, 2 * HEADS])
        gt = at("g_tok", 127.5, [P, NCHUNK, 2 * HEADS])
        vec = at("vectors", 127.75, [P, 4, KT_N])
        modc = at("mod", 128, [P, 2, 96])
        bmod = at("bmod", 128.75, [P, 96])
        taps = at("taps", 129.125, [P, HEADS, 15])
        hytaps = at("hytaps", 129.625, [P, HEADS, 12])
        small = at("small", 130, [P, 64])
        cvec = at("c_vec", 130.5, [P, 3, 2 * KT_N])
        hv = at("head_vectors", 131, [P, 6 * NCHUNK * 2])
        gst = at("g_static", 131.25, [P, 2, NCHUNK])
        ss = at("sumsq", 131.375, [P, 4, 6])
        ct = at("head_taps", 131.5, [P, 15])
        hct = at("hy_taps", 131.625, [P, 12])
        scal = at("scales", 131.75, [P, 2, 2, KT_N])
        mixf = at("mix_f32", 132, [P, HEADS, SEQ])
        x0 = at("hy_x0", 140, [P, HEADS, SEQ])
        utok = at("u_tok", 148, [P, 2, HY_CH])
        pre = at("pre_conv", 156, [P, 2, SEQ + 4])
        silu = [at("k_silu", 158.0625, [P, 2, SEQ]), at("v_silu", 160.0625, [P, 2, SEQ]), at("q_silu", 162.0625, [P, 1, SEQ])]
        zbuf = at("z_raw", 163.0625, [P, SEQ])
        cx1 = at("hy_x1", 164.0625, [P, SEQ])
        cvh = at("hy_v", 165.0625, [P, SEQ])
        zs = at("z_silu", 166.0625, [P, SEQ])
        G0_ = 167.0625
        ktok = at("k_tok", G0_, [P, NCHUNK, P])
        vtok = at("v_tok", G0_ + 2, [P, NCHUNK, P])
        kT = at("k_T", G0_ + 4, [P, NCHUNK, P])
        qT = at("q_T", G0_ + 6, [P, 2, P])
        bA, bB, bX, bT, bZ = ([at(f"{n}{d}", G0_ + 7 + 2 * q + 14 * d, [P, NCHUNK, P]) for d in range(2)]
                              for q, n in enumerate("ABXTZ"))
        att, qe, bS = ([at(f"{n}{d}", G0_ + 17 + q + 14 * d, [P, 2, P]) for d in range(2)]
                       for q, n in enumerate(("attn", "qe", "S")))
        xc = at("xc", 156, [P, KT_N, TOK])
        xsq = at("x_sq", 188, [P, 2, TOK])
        rr = at("rms", 192, [P, 3, TOK])
        rows = at("mod_rows", 198, [2, TOK])
        mraw = at("w_mod_raw", 0, [P, 8, TILE])
        mpiece = at("w_mod_piece", 201.0625, [P, 2, 512])
        macc = at("w_mod_sum", 205.0625, [P, 512])
        macc_a = at("w_mod_sum_a", 132, [P, 4, 512])
        macc_c = at("w_mod_sum_c", 188, [P, 4, 512])
        mtile = [at(f"w_mod_tile{s}", kb, [P, TILE]) for s, kb in enumerate((168, 176, 184, 192))]
        mtile_b = [at(f"w_mod_tile_b{s}", 88 + 8 * s, [P, TILE]) for s in range(4)]
        mtile_c = [at(f"w_mod_tile_c{s}", 170 + 8 * s, [P, TILE]) for s in range(2)]
        mtile_d = [at(f"w_mod_tile_d{s}", kb, [P, TILE]) for s, kb in enumerate((196, 176))]
        gb = at("gate_rows", 148, [P, 3, TOK])
        dft = at("dft", 32, [P, 4, 2, SEQ])
        kri = at("k_re_im", 40, [P, 2, 2, HY_CH])
        win = at("window", 56, [P, 2, HY_CH])
        filt = at("filt", 0, [P, 2, 2 * HY_CH])
        ab = at("taps_sum_diff", 16, [P, 2, 2, HY_CH])
        pp = at("prod", 172, [P, 2, 2, HY_CH])
        fm = at("filter_mlp", 16, [FW, 4, SEQ])
        fw = at("filter_w", 156, [FW, 3 * FW + 2 * HY_CH])
        hb0 = at("hy_bias", 40, [1, HY_CH])
        fv = at("filter_v", 207.0625, [FW, 8])
        mh = at("mix_hi", 0, [P, KT_N, SEQ], F32R)
        ml = at("mix_lo", 16, [P, KT_N, SEQ], F32R)
        hyt = at("hy_products", 156, [P, 4, 512])
        yb = at("y_buf", 164, [P, HEADS, SEQ])
        xres = at("x_res", 32, [P, KT_N, SEQ])
        ot = at("proj_out", 48, [P, KT_N, SEQ])
        r2 = at("rms2", 164, [P, 3, SEQ])
        osq = at("o_sq", 167, [P, 2, SEQ])
        h2f = at("h2_unshifted", 170, [P, KT_N, SEQ])
        h2h = at("h2_hi", 0, [P, KT_N, SEQ], F32R)
        h2l = at("h2_lo", 16, [P, KT_N, SEQ], F32R)
        fhi = at("ff_hi", 131.75, [P, FF_T, SEQ], F32R)
        flo = (at("ff_lo_a", 48, [P, 12, SEQ], F32R), at("ff_lo_b", 175.75, [P, 32, SEQ], F32R))
        fs = at("ff_silu", 60, [P, 2, SEQ])
        fa = at("ff_act", 62, [P, 2, SEQ])
        scal2 = at("scales2", 131, [P, 3, KT_N])
        dn = at("down_out", 0, [P, KT_N, SEQ])
        osq2 = at("o_sq2", 16, [P, 2, SEQ])
        r3 = at("rms3", 18, [P, 3, SEQ])
        res = at("result", 48, [P, KT_N, SEQ])
        G = [ctx.enter_context(nc.psum_tensor(f"g{i}", [P, 512], F32)) for i in range(6)]
        O = [ctx.enter_context(nc.psum_tensor(f"o{i}", [P, 512], F32)) for i in range(2)]

        GA = Phase("gates", 1, 1, [2], [1])
        H0, H = Phase("head0", 7, 1, RAW_OF_HEAD), Phase("heads", 7, 7, RAW_OF_HEAD)
        W0, W = Phase("out0", 2, 1), Phase("out", 2, 7)
        Fa0, Fa, Fb = Phase("ffa0", 4, 1, RAW_OF_4), Phase("ffa", 4, 5, RAW_OF_4), Phase("ffb", 4, 16, RAW_OF_4)
        DN = Phase("down", 8, 8)
        st = Stream([GA, H0, H, W0, W, Fa0, Fa, Fb, DN])
        st.plan()
        N_CONST, N_AUX = 10, 9
        src = {"gates": (A["w_gates_t"], 0),
               "head0": (A["w_heads_t"], 0), "heads": (A["w_heads_t"], 7), "out0": (A["w_out_t"], 0), "out": (A["w_out_t"], 2),
               "ffa0": (A["w_ff_t"], 0), "ffa": (A["w_ff_t"], 4), "ffb": (A["w_ff_t"], 24), "down": (A["w_down_t"], 0)}
        DNK = 11
        size = lambda p: DNK * P if p is DN else TILE

        landed = [sem(f"raw_landed{s}") for s in range(RAW_SLOTS)]
        hi_ready, lo_ready, w_used = sem("w_hi_ready"), sem("w_lo_ready"), sem("w_tile_used")
        c_in, consts_in, x_in, aux_in, res_in, stored = sem("c_in"), sem("consts_in"), sem("x_in"), sem("aux_in"), sem("res_in"), sem("stored")
        cs_ready, cs_act, xsq_done, xsum_done, xn_done = sem("c_ready"), sem("c_act"), sem("x_squared"), sem("x_summed"), sem("x_normed")
        xsq_used = sem("x_sq_used")
        mod_landed = [sem(f"mod_landed{s}") for s in range(8)]
        mod_used, rows_out, rows_t, mod_cols = sem("mod_tile_used"), sem("mod_rows_out"), sem("mod_rows_t"), sem("mod_cols")
        mtile_landed, mtile_done = [sem(f"mod_late_landed{s}") for s in range(4)], sem("mod_late_tile_done")
        piece_landed = [sem(f"mod_piece_landed{s}") for s in range(2)]
        piece_scaled, piece_done, macc_used = (sem("mod_piece_scaled"), sem("mod_piece_done"), sem("mod_sum_used"))
        scal_ready, hx_ready, h_hi, h_lo = sem("scales_ready"), sem("h_ctx_scaled"), sem("h_hi_ready"), sem("h_lo_ready")
        gates_act, gates_dve, gates_t = sem("gates_act"), sem("gates_dve"), sem("gates_pe")
        evac, conv_st, tanh_st, uh_t = sem("head_tile_out"), sem("conv_stage"), sem("conv_tanh"), sem("uh_transposed")
        hop_done, act_st, dve_st = sem("gdn_pe_hop"), sem("gdn_act_stage"), sem("gdn_dve_stage")
        hyp, hya, hyd, mix_lo = sem("hyena_pe"), sem("hyena_act"), sem("hyena_dve"), sem("mix_lo_ready")
        wo_free, wo_sq, wo_sum, post1 = sem("out_bank_free"), sem("out_sq"), sem("out_sq_used"), sem("res_done")
        s2_sq, s2_sum, h2_f, h2_hi, h2_lo = sem("res_sq"), sem("res_sq_used"), sem("h2_f32"), sem("h2_hi"), sem("h2_lo")
        ff_silu, ff_act, ff_hi, ff_lo = sem("ff_silu"), sem("ff_act"), sem("ff_hi"), sem("ff_lo")
        dn_free, dn_sq, dn_sum, fin = sem("down_bank_free"), sem("down_sq"), sem("down_sq_used"), sem("result_ready")

        VS = ["hv", "zs", "norm", "bv", "dmax", "A", "B0f", "B0b", "z1", "B1f", "B1b", "attn"] + [
            x for l in range(1, 7) for x in ([f"B{l + 1}f", f"B{l + 1}b"] if l < 6 else ["ks"]) + [f"L{l}f", f"L{l}b"]] + [
                  f"{w}{n}{d}" for n in range(4) for w, ds_ in (("vt", "fb"), ("s", "fb")) for d in ds_ if not (w == "s" and n == 3)
              ] + ["osum", "o", "mix"]
        AS = ["tz", "ss", "kt", "exp"] + [f"X{l}{d}" for l in range(1, 7) for d in "fb"] + [
            f"vn{n}{d}" for n in range(4) for d in "fb"] + ["of", "os"]
        CS = ["ck", "k", "cv", "v", "cq", "q", "x1", "xv", "x0"]
        HOPS = 28
        EARLY = (0, 1, 2, 4, 5, 6, 9, 10, 13, 17, 18, 21)
        PIECES = (1, 2, 3, 5, 6, 9, 10, 13, 14, 17, 18, 19, 21, 22, 23, 25)
        HOP_SLOT = (0, 3, 4, 6, 7, 8, 9, 10, 11, 12, 13, 14, 15, 16, 17, 18, 19, 19, 20, 20, 21, 21, 22, 22, 23, 23, 24, 27)
        VI, AI, CI = ({n: k for k, n in enumerate(x)} for x in (VS, AS, CS))

        def wait_conv(e, h, name):
            e.wait_ge(conv_st, h * len(CS) + (CI[name] + 1))

        def wait_dve(e, h, name):
            e.wait_ge(dve_st, h * len(VS) + (VI[name] + 1))

        def wait_act(e, h, name):
            e.wait_ge(act_st, h * len(AS) + (AI[name] + 1))

        def wait_hop(e, h, k):
            e.wait_ge(hop_done, h * HOPS + (k + 1))

        def bc(a, n=P):
            return a.unsqueeze(2).broadcast_to([a.shape[0], a.shape[1], n])

        def mid(a, m=NCHUNK):
            return a.unsqueeze(1).broadcast_to([a.shape[0], m, a.shape[1]])

        IDN, TRI, ONES = sq[:, 0], (sq[:, 1], sq[:, 2]), sq[:, 3]
        flat = lambda t: t[:].rearrange("p a b -> p (a b)")

        def newton(e, y, x, t):
            e.tensor_scalar(y.bitcast(I32), x.bitcast(I32), -0.5, float(0x5F3759DF), ALU.mult, ALU.add)
            e.drain()
            for _ in range(3):
                e.tensor_tensor(t, y, y, ALU.mult)
                e.drain()
                e.scalar_tensor_tensor(out=t, in0=t, scalar=-0.5, in1=x, op0=ALU.mult, op1=ALU.mult)
                e.drain()
                last = e.scalar_tensor_tensor(out=y, in0=t, scalar=1.5, in1=y, op0=ALU.add, op1=ALU.mult)
                e.drain()
            return last

        def split_hi(e, p, i, j):
            e.wait_ge(landed[p.raw[j]], st.landed(p, i, j))
            e.copy(whi[p.split[j]][:, :size(p)], raw[p.raw[j]][:, :size(p)]).then_inc(hi_ready, 1)

        def split_lo(e, p, i, j):
            e.wait_ge(hi_ready, st.tile(p, i, j) + 1)
            e.tensor_tensor(wlo[p.split[j]][:, :size(p)], raw[p.raw[j]][:, :size(p)],
                            whi[p.split[j]][:, :size(p)].bitcast(F32), ALU.subtract).then_inc(lo_ready, 1)

        def refill(e, split, p, i, j):
            e.wait_ge(w_used, st.tile(p, i, j) + 1)
            for u in st.refill(p, i, j):
                split(e, *u)

        def tile_done(e, p, i, j):
            e.wait_ge(w_used, st.tile(p, i, j) + 1)

        def tile_ready(e, p, i, j):
            e.wait_ge(hi_ready, st.tile(p, i, j) + 1)
            e.wait_ge(lo_ready, st.tile(p, i, j) + 1)

        def mm3(e, o, s, kk, xh, xl, first, last):
            a, b = whi[s][:, kk * P:(kk + 1) * P], wlo[s][:, kk * P:(kk + 1) * P]
            e.matmul(o, a, xh, start=first, stop=False)
            e.matmul(o, a, xl, start=False, stop=False)
            return e.matmul(o, b, xh, start=False, stop=last)

        block = ctx.enter_context(nc.Block())

        def mod_column_sum(pe, done, n, sums, bank):
            pe.wait_ge(done, n)
            for b in range(4 * len(sums)):
                last = pe.matmul(bank[:, SEQ + b:SEQ + b + 1], sums[b // 4][:, b % 4 * P:(b % 4 + 1) * P], ONES[:, 0:1],
                                 start=True, stop=True)
            last.then_inc(macc_used, 1)

        def gdn_pe(pe, h, k):
            last = None
            both = ((0, "f"), (1, "b"))
            if k == 0:
                wait_conv(pe, h, "q")
                wait_dve(pe, h, "hv")
                for c in range(NCHUNK):
                    pe.transpose(G[0][:, c * P:(c + 1) * P], silu[0][:, c // 2, (c % 2) * P:(c % 2 + 1) * P], IDN)
                for c in range(NCHUNK):
                    pe.transpose(G[1][:, c * P:(c + 1) * P], silu[1][:, c // 2, (c % 2) * P:(c % 2 + 1) * P], IDN)
                for c in range(2):
                    pe.transpose(G[2][:, c * P:(c + 1) * P], silu[2][:, 0, c * P:(c + 1) * P], IDN)
                for d in range(2):
                    for c in range(NCHUNK):
                        last = pe.matmul(G[3 + d][:, c * P:(c + 1) * P], gst[:, d, c:c + 1].broadcast_to([P, P]),
                                         TRI[d], start=True, stop=True)
            elif k == 1:
                wait_dve(pe, h, "norm")
                for c in range(NCHUNK):
                    pe.transpose(G[0][:, c * P:(c + 1) * P], ktok[:, c], IDN)
                for c in range(2):
                    last = pe.transpose(G[2][:, c * P:(c + 1) * P], bX[1][:, c], IDN)
            elif k == 2:
                wait_act(pe, h, "kt")
                wait_dve(pe, h, "bv")
                for c in range(NCHUNK):
                    pe.matmul(G[5][:, c * P:(c + 1) * P], kT[:, c], kT[:, c], start=True, stop=True)
                for c in range(2):
                    last = pe.matmul(G[1][:, c * P:(c + 1) * P], kT[:, c], qT[:, c], start=True, stop=True)
            elif k == 3:
                wait_dve(pe, h, "B0b")
                for d, _ in both:
                    for c in range(NCHUNK):
                        last = pe.matmul(G[3 * d][:, c * P:(c + 1) * P], bB[d][:, c], IDN, start=True, stop=True)
            elif k < 16:
                lv, second = 1 + (k - 4) // 2, (k - 4) % 2
                for d, n in both:
                    if not second:
                        wait_dve(pe, h, f"B{lv}{n}")
                        wait_dve(pe, h, f"L{lv - 1}{n}" if lv > 1 else "z1")
                        for c in range(NCHUNK):
                            last = pe.matmul(G[3 * d][:, c * P:(c + 1) * P], bB[d][:, c], bZ[d][:, c], start=True, stop=True)
                    else:
                        if lv == 1 and d == 0:
                            wait_dve(pe, h, "attn")
                        wait_act(pe, h, f"X{lv}{n}")
                        for c in range(NCHUNK):
                            last = pe.matmul(G[3 * d + 1][:, c * P:(c + 1) * P], bT[d][:, c], bX[d][:, c], start=True, stop=True)
                        for c in range(NCHUNK if lv < 6 else 0):
                            last = pe.matmul(G[3 * d + 2][:, c * P:(c + 1) * P], bX[d][:, c], bT[d][:, c], start=True, stop=True)
            elif k < 27:
                n, what = (0, k - 15) if k < 18 else (1 + (k - 18) // 3, (k - 18) % 3)
                for d, m in both:
                    c = ORDER[d][n]
                    if what == 0:
                        wait_dve(pe, h, f"s{n - 1}{m}")
                        last = pe.matmul(G[3 * d][:, P:2 * P], kT[:, c], bS[d][:, n % 2], start=True, stop=True)
                    elif what == 1:
                        wait_dve(pe, h, f"vt{n}{m}")
                        last = pe.matmul(G[3 * d][:, 0:P], bZ[d][:, c], bB[d][:, 0], start=True, stop=True)
                    else:
                        wait_act(pe, h, f"vn{n}{m}")
                        if c < 2:
                            oo = G[3 * d + 2][:, c * P:(c + 1) * P]
                            pe.matmul(oo, qe[d][:, c], bS[d][:, n % 2], start=True, stop=False)
                            last = pe.matmul(oo, att[d][:, c], bB[d][:, 1], start=False, stop=True)
                        if n < 3:
                            if n == 0:
                                wait_dve(pe, h, "ks")
                            last = pe.matmul(G[3 * d + 1][:, 0:P], bA[d][:, c], bB[d][:, 1], start=True, stop=True)
            else:
                wait_dve(pe, h, "o")
                for c in range(2):
                    last = pe.transpose(G[1][:, c * P:(c + 1) * P], bX[0][:, c], IDN)
            if k == 27:
                mod_column_sum(pe, piece_done, 15 * h + 15, [macc], G[1])
                pe.drain().then_inc(hop_done, 1)
            else:
                last.then_inc(hop_done, 1)

        def head_piece(pe, p, i, h, slot):
            j, q = slot // 4, slot % 4
            n = TOK if j < 2 else SEQ
            if q == 0:
                tile_ready(pe, p, i, j)
                first = isinstance(h, int) and h == 0
                if j == 0 and not first:
                    pe.wait_ge(evac, 8 * h - 1)
                elif j == 1 and not first:
                    pe.wait_ge(evac, 8 * h)
                elif j >= 2:
                    pe.wait_ge(evac, 8 * h + j - 1)
            for k in range(4 * q, 4 * q + 4):
                last = mm3(pe, O[j % 2][:, :n], p.split[j], k, hh[:, k, :n], hl[:, k, :n], k == 0, k == KT_N - 1)
            if q == 3:
                last.then_inc(w_used, 1)

        UB = ((O[0], O[1]), (G[4], G[5]))

        def transform_u(pe, q):
            ft, n = q // 2, q % 2
            for part in range(2):
                for t in range(2):
                    last = pe.matmul(UB[q % 2][part][:, :], dft[:, part, t, ft * P:(ft + 1) * P],
                                     utok[:, t, n * 512:(n + 1) * 512], start=(t == 0), stop=(t == 1))
            last.then_inc(hyp, 1)

        def filter_pe(pe, slot):
            if slot in (1, 3, 5):
                l = (slot - 1) // 2
                if l == 0:
                    pe.wait_ge(aux_in, 16 * N_AUX)
                else:
                    pe.wait_ge(hya, l)
                w, x = (fw[0:EMB, 0:FW], fm[0:EMB, 3]) if l == 0 else (fw[:, l * FW:(l + 1) * FW], fm[:, 0])
                pe.matmul(O[0][0:FW, 0:SEQ], w, x, start=True, stop=True).then_inc(hyp, 1)
            elif 7 <= slot < 15:
                t, n = (slot - 7) // 4, (slot - 7) % 4
                if slot == 7:
                    pe.wait_ge(hya, 3)
                else:
                    pe.wait_ge(hyd, max(3, slot - 5))
                pe.matmul(O[slot % 2][:, :], fm[:, 0, t * P:(t + 1) * P], fw[:, 3 * FW + n * 512:3 * FW + (n + 1) * 512],
                          start=True, stop=True).then_inc(hyp, 1)
            elif 16 <= slot < 24:
                q = slot - 16
                part, ft, n = q // 4, (q // 2) % 2, q % 2
                if q == 0:
                    pe.wait_ge(hyd, 12)
                if q >= 2:
                    pe.wait_ge(hya, q + 2)
                for t in range(2):
                    last = pe.matmul(O[q % 2][:, :], dft[:, part, t, ft * P:(ft + 1) * P], ab[:, part, t, n * 512:(n + 1) * 512],
                                     start=(t == 0), stop=(t == 1))
                last.then_inc(hyp, 1)
            elif slot == 25:
                pe.wait_ge(evac, 8 * HEADS)
                pe.wait_ge(hya, 11)
                transform_u(pe, 0)

        def gates_pe(pe, slot):
            if slot == 1:
                pe.wait_ge(gates_dve, 2)
                for c in range(NCHUNK):
                    last = pe.transpose(G[0][:, c * 64:c * 64 + 48], gb[0:48, 0, c * P:(c + 1) * P], IDN[0:48, 0:48])
                last.then_inc(gates_t, 1)
            elif slot == 3:
                pe.wait_ge(gates_dve, 3)
                for d in range(2):
                    pe.matmul(G[1][:, d * 32:(d + 1) * 32], TRI[d], gt[:, :, 8 * d:8 * d + 8], start=True, stop=True)
                pe.matmul(G[2][:, 0:64], ONES, gt[:, :, :], start=True, stop=True).then_inc(gates_t, 1)

        def head_pe(pe, p, i, h, g):
            for slot in range(28):
                if h is not None:
                    head_piece(pe, p, i, h, slot)
                if g is not None:
                    for k in range(HOPS):
                        if HOP_SLOT[k] == slot:
                            gdn_pe(pe, g, k)
                if p is H0:
                    gates_pe(pe, slot)
                if h is None:
                    filter_pe(pe, slot)
            if h is not None:
                wait_conv(pe, h, "xv")
                pe.wait_ge(evac, 8 * h + 6)
                for t in range(2):
                    last = pe.transpose(O[1][:, t * P:(t + 1) * P], cx1[:, t * P:(t + 1) * P], IDN)
                last.then_inc(uh_t, 1)

        @block.tensor
        def _(pe):
            def chunk(n, u, i):
                for j in range(4):
                    s = 4 * u + j
                    pe.wait_ge(mod_landed[s], 16 * (i + 1))
                    if j == 0 and not (isinstance(n, int) and n < 2):
                        pe.wait_ge(rows_out, n - 1)
                    for kk in range(4):
                        k = 4 * j + kk
                        last = pe.matmul(O[u][0:2, :], cvec[:, 2, 2 * k:2 * k + 2], mraw[:, s, kk * 512:(kk + 1) * 512],
                                         start=(k == 0), stop=(k == KT_N - 1))
                    last.then_inc(mod_used, 1)
                    if j == 1 and not (isinstance(n, int) and n == 0):
                        rows_to_columns(n - 1)

            def rows_to_columns(m):
                pe.wait_ge(rows_out, m + 1)
                if not (isinstance(m, int) and m == 0):
                    pe.wait_ge(mod_cols, m)
                for b in range(4):
                    last = pe.matmul(G[1][:, b * 2:(b + 1) * 2], rows[0:2, b * P:(b + 1) * P], IDN[0:2, 0:2], start=True, stop=True)
                last.then_inc(rows_t, 1)

            pe.wait_ge(cs_ready, 1)
            for u in range(2):
                chunk(u, u, 0)
            for k in range(KT_N):
                pe.wait_ge(xsq_done, k + 1)
                pe.matmul(G[0][:, :TOK], ONES, xsq[:, k % 2], start=(k == 0), stop=(k == KT_N - 1)).then_inc(xsq_used, 1)
            with pe.Fori(0, 3) as i:
                for u in range(2):
                    chunk(2 * i + 2 + u, u, i + 1)
            rows_to_columns(7)

            tile_ready(pe, GA, 0, 0)
            for k in range(KT_N):
                pe.wait_ge(h_lo, k + 1)
                last = mm3(pe, O[1][:, :TOK], GA.split[0], k, hh[:, k, :], hl[:, k, :], k == 0, k == KT_N - 1)
            last.then_inc(w_used, 1)
            head_pe(pe, H0, 0, 0, None)
            mod_column_sum(pe, mtile_done, 16, [macc_a[:, n] for n in range(4)], G[5])
            with pe.Fori(0, H.iters - 1) as i:
                head_pe(pe, H, i, i + 1, i)
            head_pe(pe, H, H.iters - 1, HEADS - 1, HEADS - 2)
            head_pe(pe, None, None, None, HEADS - 1)

            for q in range(1, 4):
                if q >= 2:
                    pe.wait_ge(hyd, 11 + q)
                transform_u(pe, q)
            pe.wait_ge(hyd, 16)
            for m in range(HEADS):
                b = G[m % 4]
                if m >= 4:
                    pe.wait_ge(hyd, 16 + m - 3)
                for q in range(4):
                    part, ft = q // 2, q % 2
                    last = pe.matmul(b[:, 0:SEQ], pp[:, part, ft, m * P:(m + 1) * P], dft[:, 2 + part, ft],
                                     start=(q == 0), stop=(q == 3))
                last.then_inc(hyp, 1)

            pe.wait_ge(mix_lo, 1)

            def out_tiles(p, i, m0):
                for j in range(2):
                    tile_ready(pe, p, i, j)
                    pe.wait_ge(wo_free, m0 + 2 * i + j + 1)
                    for k in range(KT_N):
                        if p is W0 and j == 0 and k == 8:
                            pe.wait_ge(hyd, 25)
                        last = mm3(pe, O[j][:, :SEQ], p.split[j], k, mh[:, k], ml[:, k], k == 0, k == KT_N - 1)
                    last.then_inc(w_used, 1)
                    if j or not (isinstance(i, int) and m0 == 0):
                        sum_squares(m0 + 2 * i + j - 1, (j + 1) % 2, j == 1 and m0 == 0)

            def sum_squares(m, u, first, last=False):
                pe.wait_ge(wo_sq, m + 1)
                pe.matmul(G[0][:, :SEQ], ONES, osq[:, u], start=first, stop=last).then_inc(wo_sum, 1)

            out_tiles(W0, 0, 0)
            with pe.Fori(0, W.iters) as i:
                out_tiles(W, i, 2)
            sum_squares(KT_N - 1, 1, False, True)
            mod_column_sum(pe, mtile_done, 28, [macc_c[:, n] for n in range(3)], G[2])
            for k in range(KT_N):
                pe.wait_ge(s2_sq, k + 1)
                pe.matmul(G[1][:, :SEQ], ONES, osq[:, k % 2], start=(k == 0), stop=(k == KT_N - 1)).then_inc(s2_sum, 1)


            def ff_tiles(p, i, m0):
                for j in range(4):
                    tile_ready(pe, p, i, j)
                    b = (O[0], O[1], G[2], G[3])[j]
                    pe.wait_ge(ff_act, m0 + 2 * i + j // 2 + 1)
                    for k in range(KT_N):
                        if p is Fa0 and j == 0:
                            pe.wait_ge(h2_lo, k + 1)
                        last = mm3(pe, b[:, :SEQ], p.split[j], k, h2h[:, k], h2l[:, k], k == 0, k == KT_N - 1)
                    last.then_inc(w_used, 1)

            ff_tiles(Fa0, 0, 0)
            with pe.Fori(0, Fa.iters) as i:
                ff_tiles(Fa, i, 2)
            mod_column_sum(pe, mtile_done, 32, [macc_c[:, 3]], G[4])
            with pe.Fori(0, Fb.iters) as i:
                ff_tiles(Fb, i, 12)
            pe.wait_ge(ff_lo, FF_T)
            with pe.Fori(0, DN.iters) as i:
                for j in range(8):
                    tile_ready(pe, DN, i, j)
                    b = (O[0], O[1])[j // 4]
                    if j % 4 == 0:
                        pe.wait_ge(dn_free, 2 * i + j // 4 + 1)
                    for kk in range(DNK):
                        k = (j % 4) * DNK + kk
                        lo = flo[0][:, k] if k < 12 else flo[1][:, k - 12]
                        last = mm3(pe, b[:, :SEQ], DN.split[j], kk, fhi[:, k], lo, k == 0, k == FF_T - 1)
                    last.then_inc(w_used, 1)
            for k in range(KT_N):
                pe.wait_ge(dn_sq, k + 1)
                pe.matmul(G[0][:, :SEQ], ONES, osq2[:, k % 2], start=(k == 0), stop=(k == KT_N - 1)).then_inc(dn_sum, 1)


        def mod_piece(act, n, q, acc):
            act.wait_ge(piece_landed[q % 2], 128 * n + 16 * (q // 2 + 1))
            act.activation(acc if q == 0 else mpiece[:, q % 2], mpiece[:, q % 2], ACT.Copy,
                           scale=cvec[:, 2, 2 * q:2 * q + 1]).then_inc(piece_scaled, 1)

        def gdn_act(act, h, k):
            def done(ins, name):
                ins.then_inc(act_st, 1)

            if k == -1:
                act.wait_ge(evac, 8 * h + 4)
                done(act.activation(zs[:], zbuf[:], ACT.Tanh, scale=0.5), "tz")
            elif k == 0:
                wait_hop(act, h, 0)
                for c in range(NCHUNK):
                    act.activation(bX[0][:, c], G[0][:, c * P:(c + 1) * P], ACT.Square, accum_out=ss[:, 0, c:c + 1])
                for c in range(2):
                    last = act.activation(bZ[1][:, c], G[2][:, c * P:(c + 1) * P], ACT.Square, accum_out=ss[:, 0, 4 + c:5 + c])
                done(last, "ss")
            elif k == 1:
                wait_hop(act, h, 1)
                act.copy(kT[:], G[0][:, :].rearrange("p (c n) -> p c n", c=NCHUNK))
                done(act.copy(qT[:], G[2][:, 0:SEQ].rearrange("p (c n) -> p c n", c=2)), "kt")
                wait_dve(act, h, "dmax")
                for d in range(2):
                    act.activation(bA[d][:], bA[d][:], ACT.Exp, scale=-1.0)
                    act.activation(att[d][:], att[d][:], ACT.Exp)
                    last = act.activation(qe[d][:], G[3 + d][:, 0:SEQ].rearrange("p (c n) -> p c n", c=2), ACT.Exp)
                done(last, "exp")
            elif 4 <= k < 16 and k % 2 == 0:
                wait_hop(act, h, k)
                lv = 1 + (k - 4) // 2
                for d, m in ((0, "f"), (1, "b")):
                    done(act.copy(bX[d][:], G[3 * d][:, :].rearrange("p (c n) -> p c n", c=NCHUNK)), f"X{lv}{m}")
            elif k == 16 or k in (19, 22, 25):
                wait_hop(act, h, k)
                n = 0 if k == 16 else (k - 16) // 3
                for d, m in ((0, "f"), (1, "b")):
                    done(act.copy(bB[d][:, 1], G[3 * d][:, 0:P]), f"vn{n}{m}")
            elif k == 26:
                wait_hop(act, h, 26)
                done(act.copy(bX[0][:, 0:2], G[2][:, 0:SEQ].rearrange("p (c n) -> p c n", c=2)), "of")
                wait_dve(act, h, "osum")
                for c in range(2):
                    last = act.activation(bX[1][:, c], bX[0][:, c], ACT.Square, accum_out=ss[:, 3, c:c + 1])
                done(last, "os")

        def filter_act(act, slot):
            if slot in (1, 3, 5):
                act.wait_ge(hyd, (slot + 1) // 2)
                act.activation(fm[:, 0], fm[:, 1], ACT.Sin).then_inc(hya, 1)
            elif 16 <= slot < 24:
                q = slot - 16
                part, ft, n = q // 4, (q // 2) % 2, q % 2
                act.wait_ge(hyp, 12 + q)
                act.copy(kri[:, part, ft, n * 512:(n + 1) * 512], O[q % 2][:, :]).then_inc(hya, 1)

        @block.scalar
        def _(act):
            act.dma_start(cvec[:, 0], A["c_t"]).then_inc(c_in, 16)
            act.dma_start(sq[:], A["c_sq"]).then_inc(c_in, 16)
            act.wait_ge(c_in, 32)
            act.activation(cvec[:, 1], cvec[:, 0], ACT.Tanh, scale=0.5).then_inc(cs_act, 1)
            for k in range(0, KT_N, 4):
                act.dma_start(xc[:, k:k + 4], A["xc_t"][:, k:k + 4]).then_inc(x_in, 16)
            act.dma_start(levf[:], A["c_lev"]).then_inc(consts_in, 16)
            act.dma_start(vec[:], A["norms_t"]).then_inc(consts_in, 16)
            act.dma_start(bmod[:], A["b_mod_t"]).then_inc(consts_in, 16)
            act.dma_start(taps[:], A["conv_qkv_t"]).then_inc(consts_in, 16)
            act.dma_start(hytaps[:, :, 0:9], A["conv_hy_t"]).then_inc(consts_in, 16)
            act.dma_start(hytaps[:, :, 9:12], A["conv_hy_b_t"]).then_inc(consts_in, 16)
            act.dma_start(small[32:48, 0:1], A["a_log_t"]).then_inc(consts_in, 16)
            act.dma_start(small[32:48, 1:2], A["dt_bias_t"]).then_inc(consts_in, 16)
            act.dma_start(small[:, 2:3], A["gdn_norm_t"]).then_inc(consts_in, 16)
            act.dma_start(small[:, 3:4], A["gdn_norm_t"]).then_inc(consts_in, 16)

            def rows_evac(m, u, i):
                act.wait_ge(mod_used, 8 * i + 4 * u + 4)
                if not (isinstance(m, int) and m == 0):
                    act.wait_ge(rows_t, m)
                act.copy(rows[:], O[u][0:2, :]).then_inc(rows_out, 1)

            for u in range(2):
                rows_evac(u, u, 0)
            for k in range(KT_N):
                if k == 0:
                    act.wait_ge(x_in, 16 * KT_N // 4)
                if k >= 2:
                    act.wait_ge(xsq_used, k - 1)
                act.activation(xsq[:, k % 2], xc[:, k], ACT.Square).then_inc(xsq_done, 1)
            with act.Fori(0, 3) as i:
                for u in range(2):
                    rows_evac(2 * i + 2 + u, u, i + 1)
            act.wait_ge(mtile_done, 4)
            split_hi(act, GA, 0, 0)
            split_hi(act, H0, 0, 0)

            act.wait_ge(scal_ready, 1)
            for k0 in range(0, KT_N, 4):
                for k in range(k0, k0 + 4):
                    act.activation(xc[:, k, 0:SEQ], xc[:, k, 0:SEQ], ACT.Identity, bias=modc[:, 0, k:k + 1],
                                   scale=scal[:, 0, 0, k:k + 1])
                act.drain()
                for k in range(k0, k0 + 4):
                    act.wait_ge(hx_ready, k + 1)
                    act.copy(hh[:, k], xc[:, k]).then_inc(h_hi, 1)

            refill(act, split_hi, GA, 0, 0)
            act.wait_ge(gates_dve, 1)
            act.activation(gb[0:16, 0], O[1][0:16, :TOK], ACT.Tanh, scale=0.5)
            act.activation(gb[32:48, 0], O[1][32:48, :TOK], ACT.Identity, bias=small[32:48, 1:2])
            act.activation(small[32:48, 4:5], small[32:48, 0:1], ACT.Exp)
            act.drain()
            act.activation(gb[32:48, 1], gb[32:48, 0], ACT.Abs)
            act.drain()
            act.activation(gb[32:48, 1], gb[32:48, 1], ACT.Exp, scale=-1.0)
            act.drain()
            act.activation(gb[32:48, 1], gb[32:48, 1], ACT.Ln, bias=1.0).then_inc(gates_act, 1)
            def evac_tile(p, i, h, j):
                tile_done(act, p, i, j)
                first = isinstance(h, int) and h == 0
                o = O[j % 2]
                if j == 0 and not first:
                    wait_conv(act, h - 1, "x0")
                elif j == 3 and not first:
                    wait_dve(act, h - 1, "zs")
                elif j and j != 3:
                    wait_conv(act, h, (None, "k", "v", None, "q", "x1", "xv")[j])
                if j < 2:
                    act.copy(pre[:, :, 2:2 + SEQ], o[:, :].rearrange("p (s n) -> p s n", s=2)).then_inc(evac, 1)
                elif j == 3:
                    act.copy(zbuf[:], o[:, :SEQ]).then_inc(evac, 1)
                else:
                    act.copy(pre[:, 0, 2:2 + SEQ], o[:, :SEQ]).then_inc(evac, 1)

            def conv_tanh(h, j):
                wait_conv(act, h, ("ck", "cv", "cq")[j])
                n = silu[j].shape[1]
                act.activation(pre[:, 0:n, 2:2 + SEQ], silu[j][:], ACT.Tanh, scale=0.5).then_inc(tanh_st, 1)

            def gates_act2():
                act.wait_ge(gates_dve, 4)
                act.activation(tabs[:, 4:6], tabs[:, 4:6], ACT.Exp)
                act.activation(tabs[:, 3], tabs[:, 2], ACT.Exp).then_inc(gates_act, 1)

            def head_act(p, i, h, g):
                for slot in range(28):
                    if p is H0 and slot == 4:
                        gates_act2()
                    if h is not None and slot and slot % 4 == 0:
                        refill(act, split_hi, p, i, slot // 4 - 1)
                        evac_tile(p, i, h, slot // 4 - 1)
                    if h is not None and slot in (6, 10, 14):
                        conv_tanh(h, slot // 4 - 1)
                    if g is not None:
                        if slot == 0:
                            gdn_act(act, g, -1)
                        for k in range(HOPS):
                            if HOP_SLOT[k] == slot:
                                gdn_act(act, g, k)
                        if slot in PIECES:
                            if PIECES.index(slot) == 0:
                                act.wait_ge(macc_used, g + 1)
                            mod_piece(act, g, PIECES.index(slot), macc[:])
                    if h is None:
                        filter_act(act, slot)
                if h is not None:
                    refill(act, split_hi, p, i, 6)
                    evac_tile(p, i, h, 6)
                if g is not None:
                    wait_dve(act, g, "mix")
                if h is not None:
                    act.wait_ge(uh_t, h + 1)
                    act.copy(utok[:, :, bass.ds(h * P, P)], O[1][:, 0:SEQ].rearrange("p (t n) -> p t n", t=2)).then_inc(evac, 1)

            head_act(H0, 0, 0, None)
            with act.Fori(0, H.iters - 1) as i:
                head_act(H, i, i + 1, i)
            head_act(H, H.iters - 1, HEADS - 1, HEADS - 2)
            head_act(None, None, None, HEADS - 1)

            act.copy(mh[:, 0:8], mixf[:]).then_inc(hya, 1)
            act.wait_ge(hyd, 24)
            act.copy(mh[:, 8:16], yb[:]).then_inc(hya, 1)

            act.sem_inc(wo_free, 2)

            def out_act(p, i, m0):
                for j in range(2):
                    refill(act, split_hi, p, i, j)
                    m = m0 + 2 * i + j
                    act.copy(ot[:, bass.ds(m, 1), :], O[j][:, :SEQ].unsqueeze(1))
                    if m0:
                        act.wait_ge(wo_sum, m - 1)
                    act.activation(osq[:, j], O[j][:, :SEQ], ACT.Square).then_inc(wo_sq, 1)
                    act.sem_inc(wo_free, 1)

            out_act(W0, 0, 0)
            with act.Fori(0, W.iters - 1) as i:
                out_act(W, i, 2)
            out_act(W, W.iters - 1, 2)
            for k in range(KT_N):
                act.wait_ge(post1, k + 1)
                if k == 0:
                    act.wait_ge(wo_sum, KT_N)
                if k >= 2:
                    act.wait_ge(s2_sum, k - 1)
                act.activation(osq[:, k % 2], xres[:, k], ACT.Square).then_inc(s2_sq, 1)
            for k in range(KT_N):
                act.wait_ge(h2_f, k + 1)
                act.activation(h2h[:, k], h2f[:, k], ACT.Identity, bias=modc[:, 0, 48 + k:49 + k]).then_inc(h2_hi, 1)

            act.sem_inc(ff_act, 2)

            def ff_act_(p, i, m0):
                for u in range(2):
                    m = m0 + 2 * i + u
                    refill(act, split_hi, p, i, 2 * u)
                    act.activation(fs[:, u], (O[0], G[2])[u][:, :SEQ], ACT.Silu).then_inc(ff_silu, 1)
                    refill(act, split_hi, p, i, 2 * u + 1)
                    act.wait_ge(ff_act, m + 3)
                    act.copy(fhi[:, bass.ds(m, 1), :], fa[:, u:u + 1]).then_inc(ff_hi, 1)

            ff_act_(Fa0, 0, 0)
            for p, m0 in ((Fa, 2), (Fb, 12)):
                with act.Fori(0, p.iters - 1) as i:
                    ff_act_(p, i, m0)
                ff_act_(p, p.iters - 1, m0)

            act.sem_inc(dn_free, 2)

            def dn_act(i):
                for j in range(8):
                    refill(act, split_hi, DN, i, j)
                    if j % 4 == 3:
                        act.copy(dn[:, bass.ds(2 * i + j // 4, 1), :], O[j // 4][:, :SEQ].unsqueeze(1)).then_inc(dn_free, 1)

            with act.Fori(0, DN.iters - 1) as i:
                dn_act(i)
            dn_act(DN.iters - 1)
            act.drain()
            for k in range(KT_N):
                if k >= 2:
                    act.wait_ge(dn_sum, k - 1)
                act.activation(osq2[:, k % 2], dn[:, k], ACT.Square).then_inc(dn_sq, 1)


        hvv = hv[:].rearrange("p (t c d) -> p t c d", t=6, c=NCHUNK)
        BETA, HALF_BETA, GCUM, NEG_BETA_EG, E_REM, E_LAST = range(6)
        mulv, addv, subv = ALU.mult, ALU.add, ALU.subtract

        def conv(e, dst, pre, taps_of, n, bias=None):
            w = dst.shape[-1]
            view = lambda t: pre[..., t:t + w]
            if bias is None:
                last = e.tensor_scalar(dst, view(0), taps_of(0), None, mulv)
            else:
                last = e.tensor_scalar(dst, view(0), taps_of(0), bias, mulv, addv)
            for t in range(1, n):
                e.drain()
                last = e.scalar_tensor_tensor(out=dst, in0=view(t), scalar=taps_of(t), in1=dst, op0=mulv, op1=addv)
            return last

        def two_seq(t):
            return t[:].rearrange("p (s c) n -> p s (c n)", s=2)

        def mod_tile(v, t, raw_, count, acc):
            for kk in range(4):
                k = 4 * (t % 4) + kk
                c = cvec[:, 2, 2 * k:2 * k + 1]
                part = raw_[:, kk * 512:(kk + 1) * 512]
                if kk == 0:
                    v.wait_ge(*count)
                if k == 0:
                    last = v.tensor_scalar(acc, part, c, None, mulv)
                else:
                    last = v.scalar_tensor_tensor(out=acc, in0=part, scalar=c, in1=acc, op0=mulv, op1=addv)
                if kk == 3:
                    last.then_inc(mtile_done, 1)
                v.drain()

        def modulation(v, n, chunks, count, bank):
            v.wait_ge(macc_used, count)
            w = 4 * chunks
            v.tensor_tensor(modc[:, 0, bass.ds(4 * n + 32, w)], bank[:, SEQ:SEQ + w], bmod[:, bass.ds(4 * n + 32, w)], addv)

        def level_blocks(v, lv):
            for d in range(2):
                v.tensor_tensor(bB[d][:], bA[d][:], mid(lev[:, d, lv]), mulv).then_inc(dve_st, 1)

        def gdn_dve(v, h, k):
            def done(ins):
                ins.then_inc(dve_st, 1)

            both = ((0, "f"), (1, "b"))
            if k == -1:
                v.tensor_copy(hvv.rearrange("p t c d -> p (t c) d").unsqueeze(3),
                              tabs[:].rearrange("p t c (d h) -> p (t c) d h", d=2)[:, :, :, bass.ds(h, 1)])
                done(v.tensor_copy(gst[:].unsqueeze(3),
                                   gt[:].rearrange("p c (d h) -> p d c h", d=2)[:, :, :, bass.ds(h, 1)]))
                wait_act(v, h, "tz")
                done(v.scalar_tensor_tensor(out=zs[:], in0=zs[:], scalar=1.0, in1=zbuf[:], op0=addv, op1=mulv))
            elif k == 0:
                wait_act(v, h, "ss")
                v.tensor_scalar(ss[:, 1], ss[:, 0], 0.25, EPS, mulv, addv)
                v.drain()
                newton(v, ss[:, 2], ss[:, 1], ss[:, 3])
                v.tensor_scalar(ss[:, 1, 0:4], ss[:, 2, 0:4], 0.5, None, mulv)
                v.tensor_scalar(ss[:, 1, 4:6], ss[:, 2, 4:6], 0.5 * HD ** -0.5, None, mulv)
                v.drain()
                v.tensor_tensor(ktok[:], G[0][:, :].rearrange("p (c n) -> p c n", c=NCHUNK), bc(ss[:, 1, 0:4]), mulv)
                done(v.tensor_tensor(bX[1][:, 0:2], G[2][:, 0:SEQ].rearrange("p (c n) -> p c n", c=2), bc(ss[:, 1, 4:6]), mulv))
                done(v.tensor_copy(vtok[:], G[1][:, :].rearrange("p (c n) -> p c n", c=NCHUNK)))
                for d in range(2):
                    v.tensor_tensor(bA[d][:], G[3 + d][:, :].rearrange("p (c n) -> p c n", c=NCHUNK), bc(hvv[:, GCUM, :, d]), subv)
                v.drain()
                for d in range(2):
                    v.tensor_scalar(att[d][:], bA[d][:, 0:2], 0.0, None, ALU.min)
                v.drain()
                for d in range(2):
                    last = v.tensor_scalar(bA[d][:], bA[d][:], 0.0, None, ALU.max)
                done(last)
            elif k == 2:
                wait_hop(v, h, 2)
                wait_act(v, h, "exp")
                kk = G[5][:, :].rearrange("p (c n) -> p c n", c=NCHUNK)
                for d in range(2):
                    v.tensor_tensor(bA[d][:], bA[d][:], kk, mulv)
                v.drain()
                for d in range(2):
                    last = v.tensor_tensor(bA[d][:], bA[d][:], bc(hvv[:, BETA, :, d]), mulv)
                done(last)
                v.drain()
                level_blocks(v, 0)
            elif k == 3:
                v.drain()
                for d in range(2):
                    v.tensor_tensor(bT[d][:], mid(IDN), bB[d][:], subv)
                wait_hop(v, h, 3)
                for d in range(2):
                    last = v.tensor_tensor(bZ[d][:], mid(IDN), G[3 * d][:, :].rearrange("p (c n) -> p c n", c=NCHUNK), subv)
                done(last)
                v.drain()
                level_blocks(v, 1)
                for d in range(2):
                    v.tensor_tensor(att[d][:], att[d][:], G[1][:, 0:SEQ].rearrange("p (c n) -> p c n", c=2), mulv)
                    v.tensor_tensor(qe[d][:], qe[d][:], qT[:], mulv)
                v.drain()
                for d in range(2):
                    last = v.tensor_tensor(att[d][:], att[d][:], mid(TRI[d], 2), mulv)
                done(last)
            elif 4 < k < 16 and k % 2:
                lv = 1 + (k - 4) // 2
                if lv < 6:
                    wait_hop(v, h, k - 1)
                    level_blocks(v, lv + 1)
                else:
                    v.drain()
                    for d in range(2):
                        last = v.tensor_tensor(bA[d][:], ktok[:], bc(hvv[:, E_REM, :, d]), mulv)
                    done(last)
                wait_hop(v, h, k)
                for d, _ in both:
                    last = v.tensor_tensor(bZ[d][:], bZ[d][:], G[3 * d + 1][:, :].rearrange("p (c n) -> p c n", c=NCHUNK), subv)
                    if lv < 6:
                        last = v.tensor_tensor(bT[d][:], bT[d][:], G[3 * d + 2][:, :].rearrange("p (c n) -> p c n", c=NCHUNK), subv)
                    done(last)
                if lv == 6:
                    for d, _ in both:
                        c = ORDER[d][0]
                        done(v.tensor_scalar(bB[d][:, 0], vtok[:, c], hvv[:, HALF_BETA, c, d:d + 1], None, mulv))
            elif k in (17, 20, 23):
                n = (k - 17) // 3
                wait_hop(v, h, k)
                for d, _ in both:
                    c = ORDER[d][n]
                    if n == 0:
                        done(v.tensor_copy(bS[d][:, 1], G[3 * d + 1][:, 0:P]))
                    else:
                        done(v.scalar_tensor_tensor(out=bS[d][:, (n + 1) % 2], in0=bS[d][:, n % 2],
                                                    scalar=hvv[:, E_LAST, c, d:d + 1], in1=G[3 * d + 1][:, 0:P],
                                                    op0=mulv, op1=addv))
                for d, _ in both:
                    c = ORDER[d][n + 1]
                    v.tensor_scalar(bB[d][:, 0], vtok[:, c], hvv[:, HALF_BETA, c, d:d + 1], None, mulv)
                v.drain()
            elif k in (18, 21, 24):
                n = 1 + (k - 18) // 3
                wait_hop(v, h, k)
                for d, _ in both:
                    c = ORDER[d][n]
                    done(v.scalar_tensor_tensor(out=bB[d][:, 0], in0=G[3 * d][:, P:2 * P], scalar=hvv[:, NEG_BETA_EG, c, d:d + 1],
                                                in1=bB[d][:, 0], op0=mulv, op1=addv))
            elif k == 26:
                wait_act(v, h, "of")
                done(v.tensor_tensor(bX[0][:, 0:2], bX[0][:, 0:2], G[5][:, 0:SEQ].rearrange("p (c n) -> p c n", c=2), addv))
                wait_act(v, h, "os")
                v.tensor_scalar(ss[:, 1, 0:2], ss[:, 3, 0:2], 1.0 / HD, EPS, mulv, addv)
                v.drain()
                newton(v, ss[:, 2, 0:2], ss[:, 1, 0:2], ss[:, 0, 0:2])
                done(v.tensor_tensor(bX[0][:, 0:2], bX[0][:, 0:2], bc(ss[:, 2, 0:2]), mulv))
            elif k == 27:
                wait_hop(v, h, 27)
                done(v.scalar_tensor_tensor(out=mixf[:, bass.ds(h, 1), :], in0=G[1][:, 0:SEQ].unsqueeze(1), scalar=small[:, 3:4],
                                            in1=zs[:].unsqueeze(1), op0=mulv, op1=mulv))

        def filter_dve(v, slot):
            if slot in (1, 3, 5):
                l = (slot - 1) // 2
                v.wait_ge(hyp, l + 1)
                v.tensor_scalar(fm[:, 1], O[0][0:FW, 0:SEQ], fv[:, 2 * l:2 * l + 1], fv[:, 2 * l + 1:2 * l + 2], addv, mulv)
                v.drain()
                v.tensor_scalar(fm[:, 2], fm[:, 1], 1 / (2 * np.pi), 12582912.0, mulv, addv)
                v.drain()
                v.tensor_scalar(fm[:, 2], fm[:, 2], 12582912.0, None, subv)
                for c in TWO_PI:
                    v.drain()
                    v.scalar_tensor_tensor(out=fm[:, 1], in0=fm[:, 2], scalar=-c, in1=fm[:, 1], op0=mulv, op1=addv)
                v.drain()
                v.tensor_scalar(fm[:, 1], fm[:, 1], PI_IN, -PI_IN, ALU.min, ALU.max).then_inc(hyd, 1)
            elif 7 <= slot < 15:
                t, n = (slot - 7) // 4, (slot - 7) % 4
                v.wait_ge(hyp, slot - 3)
                v.tensor_tensor(filt[:, t, n * 512:(n + 1) * 512], O[slot % 2][:, :], win[:, t, (n % 2) * 512:(n % 2 + 1) * 512],
                                mulv).then_inc(hyd, 1)
                v.drain()
                if slot == 10:
                    v.tensor_tensor(filt[0:1, 0, 0:HY_CH], filt[0:1, 0, 0:HY_CH], hb0[:], addv)
                    v.memset(filt[0:1, 0, HY_CH:], 0.0)
                    v.drain()
            elif slot == 15:
                for t in range(2):
                    v.tensor_tensor(ab[:, 0, t], filt[:, t, 0:HY_CH], filt[:, t, HY_CH:], addv)
                    last = v.tensor_tensor(ab[:, 1, t], filt[:, t, HY_CH:], filt[:, t, 0:HY_CH], subv)
                last.then_inc(hyd, 1)
                v.drain()

        @block.vector
        def _(v):
            v.wait_ge(cs_act, 1)
            v.scalar_tensor_tensor(out=cvec[:, 2], in0=cvec[:, 1], scalar=1.0, in1=cvec[:, 0], op0=addv, op1=mulv)
            v.drain()
            v.tensor_scalar(cvec[:, 2], cvec[:, 2], 0.5, None, mulv).then_inc(cs_ready, 1)
            v.wait_ge(consts_in, 16 * N_CONST)
            v.tensor_copy(lev[:], levf[:])
            v.tensor_scalar(small[:, 3:4], small[:, 2:3], 0.5, None, mulv)

            def mod_columns(m):
                v.wait_ge(rows_t, m + 1)
                v.tensor_tensor(modc[:, :, bass.ds(4 * m, 4)], G[1][:, 0:8].rearrange("p (b q) -> p q b", q=2),
                                bmod[:, bass.ds(4 * m, 4)].unsqueeze(1).broadcast_to([P, 2, 4]), addv).then_inc(mod_cols, 1)

            mod_columns(0)
            v.wait_ge(xsq_used, KT_N)
            v.tensor_scalar(rr[:, 1], G[0][:, :], 1.0 / D, EPS, mulv, addv)
            v.drain()
            newton(v, rr[:, 0], rr[:, 1], rr[:, 2])
            for k in range(KT_N):
                v.tensor_tensor(xc[:, k], xc[:, k], rr[:, 0], mulv)
            v.drain()
            v.drain()
            for m in range(1, 8):
                mod_columns(m)
                if m in (2, 3):
                    for t in (2 * m - 4, 2 * m - 3):
                        mod_tile(v, t, mtile_b[t], (mtile_landed[t], 16), macc_a[:, 0])
            split_lo(v, GA, 0, 0)
            split_lo(v, H0, 0, 0)
            v.drain()
            for s_ in range(2):
                last = v.scalar_tensor_tensor(out=scal[:, s_, 0], in0=modc[:, s_, 16:32], scalar=1.0, in1=vec[:, 0],
                                              op0=addv, op1=mulv)
            last.then_inc(scal_ready, 1)
            v.drain()
            for k in range(KT_N):
                v.tensor_scalar(xc[:, k, SEQ:TOK], xc[:, k, SEQ:TOK], scal[:, 1, 0, k:k + 1], modc[:, 1, k:k + 1],
                                mulv, addv).then_inc(hx_ready, 1)
            for k in range(KT_N):
                v.wait_ge(h_hi, k + 1)
                v.tensor_tensor(hl[:, k], xc[:, k], hh[:, k].bitcast(F32), subv).then_inc(h_lo, 1)
            v.drain()
            v.memset(gb[0:48], 0.0).then_inc(gates_dve, 1)
            refill(v, split_lo, GA, 0, 0)
            v.wait_ge(gates_act, 1)
            v.tensor_scalar(gb[0:16, 0], gb[0:16, 0], 0.5, 0.5, mulv, addv)
            v.scalar_tensor_tensor(out=gb[32:48, 1], in0=gb[32:48, 0], scalar=0.0, in1=gb[32:48, 1], op0=ALU.max, op1=addv)
            v.drain()
            v.tensor_scalar(gb[32:48, 0], gb[32:48, 1], small[32:48, 4:5], -1.0, mulv, mulv).then_inc(gates_dve, 1)
            v.memset(pre[:, :, 0:2], 0.0)
            v.memset(pre[:, :, 2 + SEQ:4 + SEQ], 0.0)
            v.drain()

            def short_conv(h, j):
                v.wait_ge(evac, 8 * h + j + 1)
                if j < 3:
                    if j == 0:
                        v.tensor_copy(ct[:].unsqueeze(1), taps[:, bass.ds(h, 1), :])
                        v.drain()
                    n = silu[j].shape[1]
                    conv(v, silu[j][:], pre[:, 0:n], lambda t: ct[:, 5 * j + t:5 * j + t + 1], KW).then_inc(conv_st, 1)
                    return
                b = j - 4
                tap = lambda t: hct[:, b * 3 + t:b * 3 + t + 1]
                bias = hct[:, 9 + b:10 + b]
                src_ = pre[:, 0, 1:3 + SEQ]
                if j == 6:
                    conv(v, x0[:, bass.ds(h, 1), :], src_.unsqueeze(1), tap, HW_, bias).then_inc(conv_st, 1)
                elif j == 4:
                    v.tensor_copy(hct[:].unsqueeze(1), hytaps[:, bass.ds(h, 1), :])
                    v.drain()
                    if not (isinstance(h, int) and h == 0):
                        v.wait_ge(uh_t, h)
                    conv(v, cx1[:], src_, tap, HW_, bias).then_inc(conv_st, 1)
                else:
                    conv(v, cvh[:], src_, tap, HW_, bias)
                    v.drain()
                    v.tensor_tensor(cx1[:], cx1[:], cvh[:], mulv).then_inc(conv_st, 1)
                v.drain()

            def conv_silu(h, j):
                v.wait_ge(tanh_st, 3 * h + (j + 1))
                n = silu[j].shape[1]
                v.scalar_tensor_tensor(out=silu[j][:], in0=pre[:, 0:n, 2:2 + SEQ], scalar=1.0, in1=silu[j][:],
                                       op0=addv, op1=mulv).then_inc(conv_st, 1)

            def gates_dve2(slot):
                if slot == 1:
                    v.wait_ge(gates_t, 1)
                    g0 = G[0][:, 0:256].rearrange("p (c n) -> p c n", c=NCHUNK)
                    v.tensor_copy(gt[:], g0[:, :, 32:48]).then_inc(gates_dve, 1)
                    v.tensor_copy(tabs[:, BETA], g0[:, :, 0:16])
                elif slot == 3:
                    v.wait_ge(gates_t, 2)
                    v.tensor_copy(tabs[:, GCUM].rearrange("p c (d h) -> p d c h", d=2),
                                  G[1][:, 0:64].rearrange("p (d c h) -> p d c h", d=2, c=NCHUNK))
                    v.drain()
                    gl = G[2][:, 0:64].rearrange("p (c n) -> p c n", c=NCHUNK)
                    v.tensor_tensor(tabs[:, E_REM], gl, tabs[:, GCUM], subv)
                    v.tensor_copy(tabs[:, E_LAST], gl).then_inc(gates_dve, 1)
                elif slot == 5:
                    v.wait_ge(gates_act, 2)
                    v.scalar_tensor_tensor(out=tabs[:, NEG_BETA_EG], in0=tabs[:, NEG_BETA_EG], scalar=-1.0, in1=tabs[:, BETA],
                                           op0=mulv, op1=mulv)
                    v.tensor_scalar(tabs[:, HALF_BETA], tabs[:, BETA], 0.5, None, mulv)

            def head_dve(p, i, h, g):
                for slot in range(28):
                    if p is H0:
                        gates_dve2(slot)
                    if g is not None:
                        if slot == 0:
                            gdn_dve(v, g, -1)
                        for k in range(HOPS):
                            if HOP_SLOT[k] == slot:
                                gdn_dve(v, g, k)
                        if h is None:
                            filter_dve(v, slot)
                        if slot == 27:
                            modulation(v, g + 4, 1, g + 2, G[1])
                    if h is not None and slot and slot % 4 == 0:
                        j = slot // 4 - 1
                        refill(v, split_lo, p, i, j)
                        if j != 3:
                            short_conv(h, j)
                    if h is not None and slot in (7, 11, 15):
                        conv_silu(h, slot // 4 - 1)
                    if g is None and slot in EARLY:
                        t = EARLY.index(slot)
                        t += 4
                        mod_tile(v, t, mtile[t % 4], (mtile_landed[t % 4], 16 * (t // 4 + 1)), macc_a[:, t // 4])
                if h is not None:
                    refill(v, split_lo, p, i, 6)
                    short_conv(h, 6)
                v.drain()

            head_dve(H0, 0, 0, None)
            modulation(v, 0, 4, 1, G[5])
            with v.Fori(0, H.iters - 1) as i:
                head_dve(H, i, i + 1, i)
            head_dve(H, H.iters - 1, HEADS - 1, HEADS - 2)
            head_dve(None, None, None, HEADS - 1)

            v.wait_ge(hya, 11)
            for q in range(4):
                ft, n = q // 2, q % 2
                v.wait_ge(hyp, 20 + q)
                kre, kim = (kri[:, a, ft, n * 512:(n + 1) * 512] for a in range(2))
                ure, us = UB[q % 2][0][:, :], UB[q % 2][1][:, :]
                v.tensor_tensor(hyt[:, 0], ure, kre, mulv)
                v.tensor_tensor(hyt[:, 1], us, kim, mulv)
                v.tensor_tensor(hyt[:, 2], ure, kim, mulv)
                v.tensor_tensor(hyt[:, 3], us, kre, mulv)
                v.drain()
                v.tensor_tensor(pp[:, 0, ft, n * 512:(n + 1) * 512], hyt[:, 0], hyt[:, 1], addv)
                v.tensor_tensor(pp[:, 1, ft, n * 512:(n + 1) * 512], hyt[:, 2], hyt[:, 3], subv).then_inc(hyd, 1)
                v.drain()
            v.wait_ge(hya, 12)
            v.tensor_tensor(ml[:, 0:8], mixf[:], mh[:, 0:8].bitcast(F32), subv).then_inc(mix_lo, 1)
            for m in range(HEADS):
                v.wait_ge(hyp, 24 + m)
                v.tensor_tensor(yb[:, m], G[m % 4][:, 0:SEQ], x0[:, m], mulv).then_inc(hyd, 1)
            v.drain()
            v.wait_ge(hya, 13)
            v.tensor_tensor(ml[:, 8:16], yb[:], mh[:, 8:16].bitcast(F32), subv).then_inc(hyd, 1)

            def late_tile(v, t, tiles):
                mod_tile(v, t, tiles[t % 2], (mtile_landed[t % 2], 16 * (t // 2 + 5)), macc_c[:, t // 4])

            for m in range(8):
                p, i = (W, m - 1) if m else (W0, 0)
                refill(v, split_lo, p, i, 0)
                late_tile(v, (3 * m + 1) // 2, mtile_c)
                refill(v, split_lo, p, i, 1)
                if m % 2 == 0:
                    late_tile(v, 3 * m // 2 + 1, mtile_c)
            v.drain()
            modulation(v, 12, 3, 10, G[2])
            v.drain()
            v.tensor_tensor(scal2[:, 0], modc[:, 0, 32:48], vec[:, 1], mulv)
            v.scalar_tensor_tensor(out=scal2[:, 1], in0=modc[:, 0, 64:80], scalar=1.0, in1=vec[:, 2], op0=addv, op1=mulv)
            v.wait_ge(wo_sum, KT_N)
            v.tensor_scalar(r2[:, 1], G[0][:, :SEQ], 1.0 / D, EPS, mulv, addv)
            v.drain()
            newton(v, r2[:, 0], r2[:, 1], r2[:, 2])
            v.wait_ge(res_in, 16)
            rb = r2[:, 0].unsqueeze(1).broadcast_to([P, 4, SEQ])
            for k in range(0, KT_N, 4):
                v.tensor_tensor(ot[:, k:k + 4], ot[:, k:k + 4], rb, mulv)
            v.drain()
            for k in range(KT_N):
                v.scalar_tensor_tensor(out=xres[:, k], in0=ot[:, k], scalar=scal2[:, 0, k:k + 1], in1=xres[:, k],
                                       op0=mulv, op1=addv).then_inc(post1, 1)
            v.wait_ge(s2_sum, KT_N)
            v.tensor_scalar(r2[:, 1], G[1][:, :SEQ], 1.0 / D, EPS, mulv, addv)
            v.drain()
            newton(v, r2[:, 0], r2[:, 1], r2[:, 2])
            for k in range(KT_N):
                v.scalar_tensor_tensor(out=h2f[:, k], in0=xres[:, k], scalar=scal2[:, 1, k:k + 1], in1=r2[:, 0],
                                       op0=mulv, op1=mulv).then_inc(h2_f, 1)
            v.drain()
            for k in range(KT_N):
                v.wait_ge(h2_hi, k + 1)
                v.scalar_tensor_tensor(out=h2l[:, k], in0=h2f[:, k], scalar=modc[:, 0, 48 + k:49 + k],
                                       in1=h2h[:, k].bitcast(F32), op0=addv, op1=subv).then_inc(h2_lo, 1)
            v.drain()

            def ff_dve(p, i, m0, lo, l0):
                for u in range(2):
                    m = m0 + 2 * i + u
                    refill(v, split_lo, p, i, 2 * u)
                    refill(v, split_lo, p, i, 2 * u + 1)
                    v.wait_ge(ff_silu, m + 1)
                    v.tensor_tensor(fa[:, u], (O[1], G[3])[u][:, :SEQ], fs[:, u], mulv).then_inc(ff_act, 1)
                    v.wait_ge(ff_hi, m + 1)
                    v.tensor_tensor(lo[:, bass.ds(m - l0, 1), :], fa[:, u:u + 1], fhi[:, bass.ds(m, 1), :].bitcast(F32),
                                    subv).then_inc(ff_lo, 1)

            for n, tiles in enumerate(((), (12,), (13,), (14,), (15,), ())):
                ff_dve(*((Fa, n - 1, 2) if n else (Fa0, 0, 0)), flo[0], 0)
                for t in tiles:
                    late_tile(v, t, mtile_d)
            modulation(v, 15, 1, 11, G[4])
            v.drain()
            v.tensor_tensor(scal2[:, 2], modc[:, 0, 80:96], vec[:, 3], mulv)
            with v.Fori(0, Fb.iters - 1) as i:
                ff_dve(Fb, i, 12, flo[1], 12)
            ff_dve(Fb, Fb.iters - 1, 12, flo[1], 12)

            def dn_dve(i):
                for j in range(8):
                    refill(v, split_lo, DN, i, j)

            with v.Fori(0, DN.iters - 1) as i:
                dn_dve(i)
            dn_dve(DN.iters - 1)
            v.wait_ge(dn_sum, KT_N)
            v.tensor_scalar(r3[:, 1], G[0][:, :SEQ], 1.0 / D, EPS, mulv, addv)
            v.drain()
            newton(v, r3[:, 0], r3[:, 1], r3[:, 2])
            for k in range(0, KT_N, 4):
                v.tensor_tensor(dn[:, k:k + 4], dn[:, k:k + 4], r3[:, 0].unsqueeze(1).broadcast_to([P, 4, SEQ]), mulv)
            v.drain()
            for k in range(KT_N):
                v.scalar_tensor_tensor(out=res[:, k], in0=dn[:, k], scalar=scal2[:, 2, k:k + 1], in1=xres[:, k],
                                       op0=mulv, op1=addv).then_inc(fin, 1)

        def mod_piece_load(g, n, q):
            g.dma_start(mpiece[:, q % 2], A["w_mod_t"][4 * n + 48 + q // 4][:, (q % 4) * 512:(q % 4 + 1) * 512]).then_inc(
                piece_landed[q % 2], 16)

        def mod_chunk(g, n, acc, ahead):
            for q in range(16):
                g.wait_ge(piece_scaled, 16 * n + (q + 1))
                if q == 0:
                    mod_piece_load(g, n, 2)
                    continue
                g.tensor_tensor(acc, acc, mpiece[:, q % 2], ALU.add).then_inc(piece_done, 1)
                g.wait_ge(piece_done, 15 * n + q)
                if q < 14:
                    mod_piece_load(g, n, q + 2)
                elif ahead:
                    mod_piece_load(g, n + 1, q - 14)

        @block.gpsimd
        def _(g):
            g.wait_ge(cs_ready, 1)
            g.wait_ge(rows_out, 1)
            for t in range(4):
                g.dma_start(mtile_b[t][:], A["w_mod_t"][32 + t]).then_inc(mtile_landed[t], 16)
            g.wait_ge(h_lo, KT_N)
            for t in range(4, 16):
                if t >= 8:
                    g.wait_ge(mtile_done, t - 3)
                g.dma_start(mtile[t % 4][:], A["w_mod_t"][32 + t]).then_inc(mtile_landed[t % 4], 16)
            for q in range(2):
                mod_piece_load(g, 0, q)
            with g.Fori(0, HEADS - 1) as i:
                mod_chunk(g, i, macc[:], True)
            mod_chunk(g, HEADS - 1, macc[:], False)
            g.wait_ge(hyd, 25)
            for t in range(16):
                if t == 12:
                    g.wait_ge(h2_lo, KT_N)
                if t >= 2:
                    g.wait_ge(mtile_done, 16 + t - 1)
                g.dma_start((mtile_c, mtile_d)[t // 12][t % 2][:], A["w_mod_t"][80 + t]).then_inc(mtile_landed[t % 2], 16)

        @block.sync
        def _(sp):
            def load(p, i, j):
                n = st.free(st.raw, p, i, j)
                if n is not None:
                    sp.wait_ge(lo_ready, n)
                a, off = src[p.name]
                idx = off + p.n * i + j
                sp.dma_start(raw[p.raw[j]][:, :size(p)], a[idx]).then_inc(landed[p.raw[j]], 16)

            def stream(p):
                if p.iters <= 2:
                    for i in range(p.iters):
                        for j in range(p.n):
                            load(p, i, j)
                else:
                    with sp.Fori(0, p.iters) as i:
                        for j in range(p.n):
                            load(p, i, j)

            def mod_load(i, s, first):
                if not first:
                    sp.wait_ge(mod_used, 8 * i + s - 7)
                sp.dma_start(mraw[:, s], A["w_mod_t"][8 * i + s]).then_inc(mod_landed[s], 16)

            sp.wait_ge(c_in, 32)
            for s in range(8):
                mod_load(0, s, True)
            with sp.Fori(0, 3) as i:
                for s in range(8):
                    mod_load(i + 1, s, False)
            for p in (GA, H0, H, W0):
                stream(p)
            tile_done(sp, H, 6, 6)
            sp.dma_start(dft[:], A["c_dft"]).then_inc(aux_in, 16)
            sp.dma_start(win[:], A["c_win"]).then_inc(aux_in, 16)
            wait_hop(sp, HEADS - 1, 0)
            wait_conv(sp, HEADS - 1, "x0")
            wait_dve(sp, HEADS - 1, "zs")
            sp.wait_ge(uh_t, HEADS)
            sp.dma_start(fw[0:EMB, 0:FW], A["filt_w1"]).then_inc(aux_in, 16)
            sp.dma_start(fw[:, FW:2 * FW], A["filt_w2"]).then_inc(aux_in, 16)
            sp.dma_start(fw[:, 2 * FW:3 * FW], A["filt_w3"]).then_inc(aux_in, 16)
            sp.dma_start(fw[:, 3 * FW:3 * FW + 2 * HY_CH], A["filt_w4"]).then_inc(aux_in, 16)
            sp.dma_start(fv[:], A["filt_v"]).then_inc(aux_in, 16)
            sp.dma_start(fm[0:EMB, 3], A["c_pos"]).then_inc(aux_in, 16)
            sp.dma_start(hb0[:], A["hyena_bias"]).then_inc(aux_in, 16)
            sp.wait_ge(hyd, 24)
            sp.dma_start(xres[:], A["xres_t"]).then_inc(res_in, 16)
            stream(W)
            for p in (Fa0, Fa, Fb, DN):
                stream(p)
            for m in range(KT_N):
                sp.wait_ge(fin, m + 1)
                sp.dma_start(out[m], res[:, m]).then_inc(stored, 16)
            sp.wait_ge(stored, 16 * KT_N)


def layouts(inputs):
    f = lambda n: np.ascontiguousarray(inputs[n], dtype=np.float32)
    c = np.ascontiguousarray
    a = {}
    kp = lambda w: w.reshape(w.shape[0] // P, P, w.shape[1])
    cols = lambda vct: c(vct.reshape(-1, P).T)

    def blocks(w):
        k, n = w.shape
        return c(w.reshape(k // P, P, n // P, P).transpose(2, 1, 0, 3).reshape(n // P, P, k))

    wm = f("w_mod")[0]
    a["w_mod_t"] = c(wm.reshape(4, 4, P, 24, 512).transpose(3, 0, 2, 1, 4).reshape(96, P, TILE))
    wi = f("w_in")[0]
    W1 = 1024
    k_, v_, q_ = wi[:, 0:W1], wi[:, W1:2 * W1], wi[:, 2 * W1:3 * W1]
    ba = wi[:, 3 * W1:3 * W1 + 32]
    z_ = wi[:, 3 * W1 + 32:4 * W1 + 32]
    hy = wi[:, 4 * W1 + 32:]
    gates = np.zeros((D, P), np.float32)
    gates[:, 0:16], gates[:, 32:48] = ba[:, 0:16], ba[:, 16:32]
    a["w_gates_t"] = blocks(gates)
    parts = [blocks(w) for w in (k_, v_, q_, z_, hy[:, W1:2 * W1], hy[:, 2 * W1:], hy[:, 0:W1])]
    a["w_heads_t"] = c(np.stack(parts, 1).reshape(56, P, TILE))
    a["w_out_t"] = blocks(f("w_out")[0])
    a["w_ff_t"] = c(np.stack([blocks(f("w_gate")[0]), blocks(f("w_up")[0])], 1).reshape(88, P, TILE))
    wd = f("w_down")[0]
    a["w_down_t"] = c(wd.reshape(4, 11, P, 16, P).transpose(3, 0, 2, 1, 4).reshape(64, P, 11 * P))
    x, ctx_ = f("x")[0], f("ctx")[0]
    xt, ct_ = kp(c(x.T)), kp(c(ctx_.T))
    a["xc_t"] = c(np.concatenate([xt, ct_], -1).transpose(1, 0, 2))
    a["xres_t"] = c(xt.transpose(1, 0, 2))
    a["c_t"] = c(np.stack([cols(f("c")[0]), cols(f("c_ctx"))], -1).reshape(P, 2 * KT_N))
    a["norms_t"] = c(np.stack([cols(f(n)[0]) for n in ("norm_pre_mix", "norm_post_mix", "norm_pre_ffn", "norm_post_ffn")], 1))
    a["b_mod_t"] = cols(f("b_mod")[0])
    cq = f("conv_qkv")[0].reshape(KW, 3, HEADS, P)
    a["conv_qkv_t"] = c(cq.transpose(3, 2, 1, 0).reshape(P, HEADS, 15))
    chy = f("conv_hy")[0].reshape(HW_, 3, HEADS, P)[:, [1, 2, 0]]
    a["conv_hy_t"] = c(chy.transpose(3, 2, 1, 0).reshape(P, HEADS, 9))
    a["conv_hy_b_t"] = c(f("conv_hy_b")[0].reshape(3, HEADS, P)[[1, 2, 0]].transpose(2, 1, 0))
    a["a_log_t"] = c(f("a_log")[0].reshape(16, 1))
    a["dt_bias_t"] = c(f("dt_bias")[0].reshape(16, 1))
    a["gdn_norm_t"] = c(f("gdn_norm")[0].reshape(P, 1))
    for n in ("filt_w1", "filt_w2", "filt_w3", "filt_w4"):
        a[n] = f(n)[0]
    a["filt_v"] = c(np.stack([f(n)[0] for n in ("filt_b1", "filt_freq1", "filt_b2", "filt_freq2", "filt_b3", "filt_freq3")]
                             + [f("filt_b1")[0]] * 2, 1))
    a["hyena_bias"] = f("hyena_bias")
    a.update(host_constants())
    return a


def kernel(**inputs):
    import concourse.bacc as bacc
    from concourse.bass_utils import run_bass_kernel_spmd

    arrays = layouts(inputs)
    nc = bacc.Bacc("TRN2", target_bir_lowering=False, num_devices=1)
    aps = {n: nc.dram_tensor(f"in_{n}", a.shape, mybir.dt.from_np(a.dtype), kind="ExternalInput").ap()
           for n, a in arrays.items()}
    out = nc.dram_tensor("out_0", (KT_N, P, SEQ), F32, kind="ExternalOutput").ap()
    build(nc, aps, out)
    r = run_bass_kernel_spmd(nc, [{f"in_{n}": a for n, a in arrays.items()}], core_ids=[0])
    o = r.results[0]["out_0"]
    return np.ascontiguousarray(o.transpose(2, 0, 1).reshape(1, SEQ, D))
```
